# Optimizing a Trainium2 kernel written in Bass

```python
import math
import jax, jax.numpy as jnp
from jax import lax
import numpy as np

D_MODEL = 1024
BATCH = 1
SEQ = 512
DEPTH = 1

HEAD_DIM = 64
A_HEADS = 6
A_BRANCHES = ((128, 1), (512, 4), (2048, 16))
B_HEADS = 4
B_KEY_DIM = 32
B_VAL_DIM = 64
B_GATE_RANK = 16
B_GATE_TAU = 16.0
B_CHUNK = 16
C_HEADS = 6
C_BLOCK = 256
C_TOPK = 3
C_QCHUNK = 16
REL_BUCKETS = 32
REL_MAX_DIST = 2048
D_FF = 4 * D_MODEL
EPS = 1e-6
NEG_INF = -1e30

A_WIDTH = A_HEADS * HEAD_DIM
B_QK = B_HEADS * B_KEY_DIM
B_WIDTH = B_HEADS * B_VAL_DIM
C_WIDTH = C_HEADS * HEAD_DIM
MIX_WIDTH = A_WIDTH + B_WIDTH + C_WIDTH
IN_SIZES = (A_WIDTH, A_WIDTH, A_WIDTH, B_QK, B_QK, B_WIDTH, B_WIDTH, B_GATE_RANK, C_WIDTH, C_WIDTH, C_WIDTH)
IN_WIDTH = sum(IN_SIZES)


def rmsnorm(x, w):
    xf = x.astype(jnp.float32)
    y = xf * lax.rsqrt(jnp.mean(xf * xf, axis=-1, keepdims=True) + EPS)
    return (y * w.astype(jnp.float32)).astype(x.dtype)

def rel_bucket(dist):
    n = jnp.maximum(dist, 0)
    exact = REL_BUCKETS // 2
    logv = jnp.log(jnp.maximum(n, 1).astype(jnp.float32) / exact) / math.log(REL_MAX_DIST / exact)
    large = jnp.minimum(exact + (logv * (REL_BUCKETS - exact)).astype(jnp.int32), REL_BUCKETS - 1)
    return jnp.where(n < exact, n, large)

def dilated_branch(q, k, v, bias_a, window, dilation):
    Bsz, S, H, Dh = q.shape
    L = S // dilation
    span = window // dilation
    blk = min(span, L)
    nb = -(-L // blk)
    Lp = nb * blk

    def sub(t):
        t = t.reshape(Bsz, L, dilation, H, Dh).transpose(0, 2, 1, 3, 4)
        t = jnp.pad(t, ((0, 0), (0, 0), (0, Lp - L), (0, 0), (0, 0)))
        return t.reshape(Bsz, dilation, nb, blk, H, Dh)

    def with_prev(t):
        prev = jnp.pad(t, ((0, 0), (0, 0), (1, 0), (0, 0), (0, 0), (0, 0)))[:, :, :-1]
        return jnp.concatenate([prev, t], axis=3)

    qb = sub(q)
    kc = with_prev(sub(k))
    vc = with_prev(sub(v))
    logits = jnp.einsum('brnqhe,brnkhe->brnhqk', qb, kc, preferred_element_type=jnp.float32) * (Dh ** -0.5)

    steps = jnp.arange(blk)[:, None] + blk - jnp.arange(2 * blk)[None, :]
    band = (steps >= 0) & (steps <= span)
    key_ok = (jnp.arange(nb)[:, None] * blk + jnp.arange(2 * blk)[None, :] - blk) >= 0
    mask = band[None] & key_ok[:, None, :]
    bias = bias_a[:, rel_bucket(steps * dilation)].astype(jnp.float32)
    logits = jnp.where(mask[None, None, :, None], logits + bias[None, None, None], NEG_INF)

    lse = jax.nn.logsumexp(logits, axis=-1)
    p = jnp.exp(logits - lse[..., None])
    out = jnp.einsum('brnhqk,brnkhe->brnqhe', p.astype(v.dtype), vc)
    out = out.reshape(Bsz, dilation, Lp, H, Dh)[:, :, :L].transpose(0, 2, 1, 3, 4).reshape(Bsz, S, H, Dh)
    lse = lse.transpose(0, 1, 2, 4, 3).reshape(Bsz, dilation, Lp, H)[:, :, :L].transpose(0, 2, 1, 3).reshape(Bsz, S, H)
    return out.astype(jnp.float32), lse

def dilated_attention(q, k, v, bias_a):
    outs, lses = [], []
    for window, dilation in A_BRANCHES:
        o, l = dilated_branch(q, k, v, bias_a, window, dilation)
        outs.append(o)
        lses.append(l)
    wts = jax.nn.softmax(jnp.stack(lses), axis=0)
    out = jnp.einsum('gbsh,gbshe->bshe', wts, jnp.stack(outs))
    return out.astype(q.dtype)

def gla(q, k, v, r, a_lr, w_a2, b_a, norm_w):
    f32 = jnp.float32
    Bsz, S, H, dk = q.shape
    dv = v.shape[-1]
    C = B_CHUNK
    N = S // C
    log_a = jax.nn.log_sigmoid((a_lr @ w_a2 + b_a).astype(f32)) / B_GATE_TAU

    def chunks(t):
        return t.astype(f32).reshape(Bsz, N, C, H, -1).transpose(0, 3, 1, 2, 4)

    qc = chunks(q) * (dk ** -0.5)
    kc = chunks(k)
    vc = chunks(v)
    b = jnp.cumsum(chunks(log_a.reshape(Bsz, S, H, dk)), axis=3)

    causal = jnp.tril(jnp.ones((C, C), dtype=bool))
    diff = b[..., :, None, :] - b[..., None, :, :]
    decay = jnp.exp(jnp.where(causal[:, :, None], diff, NEG_INF))
    attn = jnp.einsum('bhnic,bhnjc,bhnijc->bhnij', qc, kc, decay)
    o_intra = jnp.einsum('bhnij,bhnjv->bhniv', attn, vc)

    b_last = b[..., -1, :]
    u = jnp.einsum('bhnjc,bhnjv->bhncv', kc * jnp.exp(b_last[..., None, :] - b), vc)

    def step(state, inp):
        dec, uu = inp
        return dec[..., None] * state + uu, state

    _, s_prev = lax.scan(step, jnp.zeros((Bsz, H, dk, dv), f32),
                         (jnp.moveaxis(jnp.exp(b_last), 2, 0), jnp.moveaxis(u, 2, 0)))
    s_prev = jnp.moveaxis(s_prev, 0, 2)
    o_inter = jnp.einsum('bhnic,bhncv->bhniv', qc * jnp.exp(b), s_prev)

    o = (o_intra + o_inter).transpose(0, 2, 3, 1, 4).reshape(Bsz, S, H, dv)
    o = o * lax.rsqrt(jnp.mean(o * o, axis=-1, keepdims=True) + EPS)
    o = o.reshape(Bsz, S, H * dv) * norm_w.astype(f32) * jax.nn.silu(r.astype(f32))
    return o.astype(q.dtype)

def moba_attention(q, k, v, bias_c):
    f32 = jnp.float32
    Bsz, S, H, Dh = q.shape
    nblk = -(-S // C_BLOCK)
    Sp = nblk * C_BLOCK

    def pad(t):
        return jnp.pad(t, ((0, 0), (0, Sp - S), (0, 0), (0, 0))).transpose(0, 2, 1, 3)

    qp, kp, vp = pad(q), pad(k), pad(v)
    kb = kp.reshape(Bsz, H, nblk, C_BLOCK, Dh)
    vb = vp.reshape(Bsz, H, nblk, C_BLOCK, Dh)
    k_mean = jnp.mean(kb.astype(f32), axis=3)

    qblk = jnp.arange(Sp) // C_BLOCK
    past = jnp.arange(nblk)[None, :] < qblk[:, None]
    gate = jnp.where(past, jnp.einsum('bhsd,bhnd->bhsn', qp.astype(f32), k_mean), NEG_INF)
    topk = min(C_TOPK, nblk)
    _, idx = lax.top_k(gate, topk)
    valid = idx < qblk[None, None, :, None]

    n_q = Sp // C_QCHUNK
    qch = qp.reshape(Bsz, H, n_q, C_QCHUNK, Dh).transpose(2, 0, 1, 3, 4)
    idxch = idx.reshape(Bsz, H, n_q, C_QCHUNK, topk).transpose(2, 0, 1, 3, 4)
    valch = valid.reshape(Bsz, H, n_q, C_QCHUNK, topk).transpose(2, 0, 1, 3, 4)
    b_ix = jnp.arange(Bsz)[:, None, None, None]
    h_ix = jnp.arange(H)[None, :, None, None]
    scale = Dh ** -0.5
    nsel = topk * C_BLOCK

    def one_chunk(args):
        ci, qc_, idx_, val_ = args
        qpos = ci * C_QCHUNK + jnp.arange(C_QCHUNK)
        ksel = kb[b_ix, h_ix, idx_].reshape(Bsz, H, C_QCHUNK, nsel, Dh)
        vsel = vb[b_ix, h_ix, idx_].reshape(Bsz, H, C_QCHUNK, nsel, Dh)
        kpos = (idx_[..., None] * C_BLOCK + jnp.arange(C_BLOCK)).reshape(Bsz, H, C_QCHUNK, nsel)
        l_sel = jnp.einsum('bhqd,bhqkd->bhqk', qc_, ksel, preferred_element_type=f32) * scale
        l_sel = l_sel + bias_c[h_ix, rel_bucket(qpos[None, None, :, None] - kpos)].astype(f32)
        l_sel = jnp.where(jnp.repeat(val_, C_BLOCK, axis=-1), l_sel, NEG_INF)
        own = (ci * C_QCHUNK) // C_BLOCK
        kown = lax.dynamic_slice_in_dim(kp, own * C_BLOCK, C_BLOCK, axis=2)
        vown = lax.dynamic_slice_in_dim(vp, own * C_BLOCK, C_BLOCK, axis=2)
        d_own = qpos[:, None] - (own * C_BLOCK + jnp.arange(C_BLOCK))[None, :]
        l_own = jnp.einsum('bhqd,bhkd->bhqk', qc_, kown, preferred_element_type=f32) * scale
        l_own = jnp.where(d_own[None, None] >= 0, l_own + bias_c[:, rel_bucket(d_own)].astype(f32)[None], NEG_INF)
        p = jax.nn.softmax(jnp.concatenate([l_sel, l_own], axis=-1), axis=-1)
        out = (jnp.einsum('bhqk,bhqkd->bhqd', p[..., :nsel].astype(vsel.dtype), vsel)
               + jnp.einsum('bhqk,bhkd->bhqd', p[..., nsel:].astype(vown.dtype), vown))
        return out

    outs = lax.map(one_chunk, (jnp.arange(n_q), qch, idxch, valch))
    return outs.transpose(1, 0, 3, 2, 4).reshape(Bsz, Sp, H, Dh)[:, :S]

def hybrid_layer(x, norm1_w, w_in, w_a2, b_a, gla_norm_w, w_out, norm2_w, w_ff1, w_ff2, rel_bias):
    Bsz, S, _ = x.shape
    h = rmsnorm(x, norm1_w)
    proj = h @ w_in
    aq, ak, av, bq, bk, bv, br, ba, cq, ck, cv = jnp.split(proj, list(np.cumsum(IN_SIZES)[:-1]), axis=-1)

    def heads(t, n):
        return t.reshape(Bsz, S, n, -1)

    bias_a = rel_bias[:, :A_HEADS].T
    bias_c = rel_bias[:, A_HEADS:].T
    y_a = dilated_attention(heads(aq, A_HEADS), heads(ak, A_HEADS), heads(av, A_HEADS), bias_a)
    y_b = gla(heads(bq, B_HEADS), heads(bk, B_HEADS), heads(bv, B_HEADS), br, ba, w_a2, b_a, gla_norm_w)
    y_c = moba_attention(heads(cq, C_HEADS), heads(ck, C_HEADS), heads(cv, C_HEADS), bias_c)
    mix = jnp.concatenate([y_a.reshape(Bsz, S, A_WIDTH), y_b, y_c.reshape(Bsz, S, C_WIDTH)], axis=-1)
    x = x + mix @ w_out

    h2 = rmsnorm(x, norm2_w)
    x = x + jnp.square(jax.nn.relu(h2 @ w_ff1)) @ w_ff2
    return x

def first_inputs(seed: int = 0) -> dict:
    key = jax.random.key(seed)
    ks = jax.random.split(key, 14)
    f32 = jnp.float32
    nrm = lambda k, shape, s: (jax.random.normal(k, shape, f32) * s)
    return {
        "x": nrm(ks[0], (BATCH, SEQ, D_MODEL), 1.0),
        "norm1_w": 1.0 + nrm(ks[1], (DEPTH, D_MODEL), 0.02),
        "w_in": nrm(ks[2], (DEPTH, D_MODEL, IN_WIDTH), D_MODEL ** -0.5),
        "gla_w_a2": nrm(ks[3], (DEPTH, B_GATE_RANK, B_QK), B_GATE_RANK ** -0.5),
        "gla_b_a": nrm(ks[4], (DEPTH, B_QK), 0.1),
        "gla_norm_w": 1.0 + nrm(ks[5], (DEPTH, B_WIDTH), 0.02),
        "w_out": nrm(ks[6], (DEPTH, MIX_WIDTH, D_MODEL), MIX_WIDTH ** -0.5),
        "norm2_w": 1.0 + nrm(ks[7], (DEPTH, D_MODEL), 0.02),
        "w_ff1": nrm(ks[8], (DEPTH, D_MODEL, D_FF), D_MODEL ** -0.5),
        "w_ff2": nrm(ks[9], (DEPTH, D_FF, D_MODEL), D_FF ** -0.5),
        "rel_bias": nrm(ks[10], (REL_BUCKETS, A_HEADS + C_HEADS), 0.2),
        "final_norm_w": 1.0 + nrm(ks[11], (D_MODEL,), 0.02),
    }

def first_block(x, norm1_w, w_in, gla_w_a2, gla_b_a, gla_norm_w, w_out, norm2_w, w_ff1, w_ff2, rel_bias, final_norm_w):
    for i in range(DEPTH):
        x = hybrid_layer(x, norm1_w[i], w_in[i], gla_w_a2[i], gla_b_a[i], gla_norm_w[i], w_out[i],
                         norm2_w[i], w_ff1[i], w_ff2[i], rel_bias)
    return rmsnorm(x, final_norm_w)


DEPTH_2 = 2

CTX_LEN = 256
GRID_W = 64

FOURIER_GROUPS = 4
FOURIER_GD = 64
FOURIER_W = FOURIER_GROUPS * FOURIER_GD
ATT_HEADS = 8
ATT_KV_HEADS = 2
ATT_GROUP = ATT_HEADS // ATT_KV_HEADS
ATT_W = ATT_HEADS * HEAD_DIM
ATT_KV_W = ATT_KV_HEADS * HEAD_DIM
HG_HEADS = 4
HG_DK = 64
HG_DV = 64
HG_W = HG_HEADS * HG_DK
MIX_W = FOURIER_W + ATT_W + HG_W

OFF_FOURIER = 0
OFF_Q = OFF_FOURIER + FOURIER_W
OFF_K = OFF_Q + ATT_W
OFF_V = OFF_K + ATT_KV_W
OFF_FF = OFF_V + ATT_KV_W
OFF_FB = OFF_FF + HG_W
OFF_I = OFF_FB + HG_W
OFF_HQ = OFF_I + HG_W
OFF_G = OFF_HQ + HG_W
PROJ_W = OFF_G + HG_W

D_FF_2 = -(-8 * D_MODEL // (3 * 256)) * 256
ROPE_THETA = 10000.0
Q_BLOCK = 128
HG_CHUNK = 64


def rmsnorm_2(x, gain=None):
    xf = x.astype(jnp.float32)
    y = xf * lax.rsqrt(jnp.mean(xf * xf, axis=-1, keepdims=True) + EPS)
    if gain is not None:
        y = y * gain.astype(jnp.float32)
    return y.astype(x.dtype)

def col(u, off, width, base=0):
    return u[..., off - base: off - base + width]

def axial_rope_tables(n):
    rows = n // GRID_W
    row = jnp.repeat(jnp.arange(rows), GRID_W).astype(jnp.float32)
    colp = jnp.tile(jnp.arange(GRID_W), rows).astype(jnp.float32)
    half = HEAD_DIM // 2
    freqs = ROPE_THETA ** (-jnp.arange(0, half, 2, dtype=jnp.float32) / half)
    ang_r = row[:, None] * freqs
    ang_c = colp[:, None] * freqs
    return (jnp.cos(ang_r), jnp.sin(ang_r), jnp.cos(ang_c), jnp.sin(ang_c))

def rope_axis(x, cos, sin):
    x1, x2 = jnp.split(x, 2, axis=-1)
    return jnp.concatenate([x1 * cos - x2 * sin, x1 * sin + x2 * cos], axis=-1)

def apply_axial_rope(x, tabs):
    cr, sr, cc, sc = tabs
    xf = x.astype(jnp.float32)
    xr, xc = jnp.split(xf, 2, axis=-1)
    return jnp.concatenate([rope_axis(xr, cr, sr), rope_axis(xc, cc, sc)], axis=-1).astype(x.dtype)

def fourier_mix(u, w):
    b, n, _ = u.shape
    z = u.astype(jnp.float32).reshape(b, n, FOURIER_GROUPS, FOURIER_GD)
    z = jnp.fft.fftn(z, axes=(1, 3), norm="ortho").real
    return z.reshape(b, n, FOURIER_W).astype(u.dtype) @ w

def attend(q, k, v):
    s = jnp.einsum('bkgqd,bksd->bkgqs', q, k).astype(jnp.float32) * (HEAD_DIM ** -0.5)
    p = jax.nn.softmax(s, axis=-1).astype(v.dtype)
    return jnp.einsum('bkgqs,bksd->bkgqd', p, v)

def attend_blocked(q, k, v):
    b, kh, g, n, d = q.shape
    nb = n // Q_BLOCK
    qb = jnp.moveaxis(q.reshape(b, kh, g, nb, Q_BLOCK, d), 3, 0)
    ob = lax.map(lambda qi: attend(qi, k, v), qb)
    return jnp.moveaxis(ob, 0, 3).reshape(b, kh, g, n, d)

def q_heads(u, gain):
    b, n, _ = u.shape
    return rmsnorm_2(u.reshape(b, n, ATT_HEADS, HEAD_DIM), gain).transpose(0, 2, 1, 3)

def kv_heads(u, gain=None):
    b, n, _ = u.shape
    return rmsnorm_2(u.reshape(b, n, ATT_KV_HEADS, HEAD_DIM), gain).transpose(0, 2, 1, 3) if gain is not None \
        else u.reshape(b, n, ATT_KV_HEADS, HEAD_DIM).transpose(0, 2, 1, 3)

def group_q(qh):
    b, h, n, d = qh.shape
    return qh.reshape(b, ATT_KV_HEADS, ATT_GROUP, n, d)

def ungroup(o):
    b, kh, g, n, d = o.shape
    return o.transpose(0, 3, 1, 2, 4).reshape(b, n, kh * g * d)

def attention_group(ux, uc, base_c, q_gain, k_gain, tabs, ctx_out):
    qx = group_q(apply_axial_rope(q_heads(col(ux, OFF_Q, ATT_W), q_gain), tabs))
    kx = apply_axial_rope(kv_heads(col(ux, OFF_K, ATT_KV_W), k_gain), tabs)
    vx = kv_heads(col(ux, OFF_V, ATT_KV_W))
    kc = kv_heads(col(uc, OFF_K, ATT_KV_W, base_c), k_gain)
    vc = kv_heads(col(uc, OFF_V, ATT_KV_W, base_c))
    k_all = jnp.concatenate([kc, kx], axis=2)
    v_all = jnp.concatenate([vc, vx], axis=2)
    out_x = ungroup(attend_blocked(qx, k_all, v_all))
    out_c = None
    if ctx_out:
        qc = group_q(q_heads(col(uc, OFF_Q, ATT_W, base_c), q_gain))
        out_c = ungroup(attend(qc, kc, vc))
    return out_x, out_c

def hgrn_scan(k, v, log_f, s0, q=None):
    b, h, n, dk = k.shape
    nc = n // HG_CHUNK
    with_out = q is not None

    def chunks(a):
        return jnp.moveaxis(a.reshape(b, h, nc, HG_CHUNK, a.shape[-1]), 2, 0)

    mask = jnp.tril(jnp.ones((HG_CHUNK, HG_CHUNK), dtype=bool))[:, :, None]

    def step(s, inp):
        kc, vc, lf = inp[0], inp[1], inp[2]
        cum = jnp.cumsum(lf, axis=2)
        last = cum[:, :, -1:, :]
        s_new = jnp.exp(last[:, :, 0, :])[..., None] * s + \
            jnp.einsum('bhsd,bhse->bhde', kc * jnp.exp(last - cum), vc)
        if not with_out:
            return s_new, None
        qc = inp[3]
        o_inter = jnp.einsum('bhtd,bhde->bhte', qc * jnp.exp(cum), s)
        diff = cum[:, :, :, None, :] - cum[:, :, None, :, :]
        decay = jnp.exp(jnp.where(mask, diff, -jnp.inf))
        att = jnp.einsum('bhtd,bhsd,bhtsd->bhts', qc, kc, decay)
        return s_new, o_inter + jnp.einsum('bhts,bhse->bhte', att, vc)

    xs = (chunks(k), chunks(v), chunks(log_f)) + ((chunks(q),) if with_out else ())
    s_fin, o = lax.scan(step, s0, xs)
    if with_out:
        o = jnp.moveaxis(o, 0, 2).reshape(b, h, n, v.shape[-1])
    return o, s_fin

def hg_heads(u):
    b, n, _ = u.shape
    return u.reshape(b, n, HG_HEADS, -1).transpose(0, 2, 1, 3).astype(jnp.float32)

def hg_gate(z, lb):
    lb = lb.reshape(HG_HEADS, 1, HG_DK)
    k = (1.0 - lb) * jax.nn.sigmoid(-z)
    log_f = jnp.log(lb + (1.0 - lb) * jax.nn.sigmoid(z))
    return k, log_f

def hg_readout(o, g, gain, dtype):
    b, h, n, dv = o.shape
    y = rmsnorm_2(o, gain).transpose(0, 2, 1, 3).reshape(b, n, h * dv)
    return (y * jax.nn.silu(g.astype(jnp.float32))).astype(dtype)

def hgrn_group(ux, uc, base_c, lb_dirs, gain, ctx_out):
    b = ux.shape[0]
    vx = hg_heads(col(ux, OFF_I, HG_W))
    qx = hg_heads(col(ux, OFF_HQ, HG_W))
    vc = hg_heads(col(uc, OFF_I, HG_W, base_c))
    qc = hg_heads(col(uc, OFF_HQ, HG_W, base_c)) if ctx_out else None
    s0 = jnp.zeros((b, HG_HEADS, HG_DK, HG_DV), jnp.float32)
    o_x = jnp.zeros_like(vx)
    o_c = jnp.zeros_like(vc) if ctx_out else None
    for d, (off, rev) in enumerate(((OFF_FF, False), (OFF_FB, True))):
        fl = (lambda a: jnp.flip(a, axis=2)) if rev else (lambda a: a)
        kx, lfx = hg_gate(hg_heads(col(ux, off, HG_W)), lb_dirs[d])
        kc, lfc = hg_gate(hg_heads(col(uc, off, HG_W, base_c)), lb_dirs[d])
        oc, s_ctx = hgrn_scan(fl(kc), fl(vc), fl(lfc), s0, fl(qc) if ctx_out else None)
        ox, _ = hgrn_scan(fl(kx), fl(vx), fl(lfx), s_ctx, fl(qx))
        o_x = o_x + fl(ox)
        if ctx_out:
            o_c = o_c + fl(oc)
    out_x = hg_readout(o_x, col(ux, OFF_G, HG_W), gain, ux.dtype)
    out_c = hg_readout(o_c, col(uc, OFF_G, HG_W, base_c), gain, uc.dtype) if ctx_out else None
    return out_x, out_c

def swiglu(h, wg, wu, wd):
    return (jax.nn.silu(h @ wg) * (h @ wu)) @ wd

def second_inputs(seed: int = 0) -> dict:
    key = jax.random.key(seed)
    ks = jax.random.split(key, 18)
    nrm = jax.random.normal
    f32 = jnp.float32
    return {
        "x": nrm(ks[0], (BATCH, SEQ, D_MODEL), f32),
        "c": nrm(ks[1], (BATCH, D_MODEL), f32),
        "ctx": nrm(ks[2], (BATCH, CTX_LEN, D_MODEL), f32),
        "c_ctx": nrm(ks[3], (D_MODEL,), f32),
        "w_ada": nrm(ks[4], (DEPTH_2, D_MODEL, 6 * D_MODEL), f32) * D_MODEL ** -0.5,
        "b_ada": nrm(ks[5], (DEPTH_2, 6 * D_MODEL), f32) * 0.02,
        "w_in": nrm(ks[6], (DEPTH_2, D_MODEL, PROJ_W), f32) * D_MODEL ** -0.5,
        "w_four": nrm(ks[7], (DEPTH_2, FOURIER_W, FOURIER_W), f32) * FOURIER_W ** -0.5,
        "q_norm": 1.0 + 0.02 * nrm(ks[8], (DEPTH_2, HEAD_DIM), f32),
        "k_norm": 1.0 + 0.02 * nrm(ks[9], (DEPTH_2, HEAD_DIM), f32),
        "hg_lb_logits": 0.5 * nrm(ks[10], (2, DEPTH_2, HG_W), f32),
        "hg_norm": 1.0 + 0.02 * nrm(ks[11], (DEPTH_2, HG_DV), f32),
        "w_out": nrm(ks[12], (DEPTH_2, MIX_W, D_MODEL), f32) * MIX_W ** -0.5,
        "w_gate": nrm(ks[13], (DEPTH_2, D_MODEL, D_FF_2), f32) * D_MODEL ** -0.5,
        "w_up": nrm(ks[14], (DEPTH_2, D_MODEL, D_FF_2), f32) * D_MODEL ** -0.5,
        "w_down": nrm(ks[15], (DEPTH_2, D_FF_2, D_MODEL), f32) * D_FF_2 ** -0.5,
        "final_norm": 1.0 + 0.02 * nrm(ks[16], (D_MODEL,), f32),
    }

def second_block(x, c, ctx, c_ctx, w_ada, b_ada, w_in, w_four, q_norm, k_norm,
              hg_lb_logits, hg_norm, w_out, w_gate, w_up, w_down, final_norm):
    d = D_MODEL
    tabs = axial_rope_tables(x.shape[1])
    silu_c = jax.nn.silu(c)
    silu_cc = jax.nn.silu(c_ctx)
    lb_sm = jax.nn.softmax(hg_lb_logits.astype(jnp.float32), axis=1)
    lb_all = jnp.cumsum(lb_sm, axis=1) - lb_sm[:, :1]
    for l in range(DEPTH_2):
        ctx_out = l < DEPTH_2 - 1
        mod = silu_c @ w_ada[l] + b_ada[l]
        sh_a, sc_a, g_a, sh_f, sc_f, g_f = jnp.split(mod[:, None, :], 6, axis=-1)
        n_c = 6 * d if ctx_out else 2 * d
        mc = jnp.split(silu_cc @ w_ada[l][:, :n_c] + b_ada[l][:n_c], n_c // d)
        hx = rmsnorm_2(x) * (1 + sc_a) + sh_a
        hc = rmsnorm_2(ctx) * (1 + mc[1]) + mc[0]
        ux = hx @ w_in[l]
        base_c = 0 if ctx_out else OFF_K
        uc = hc @ (w_in[l] if ctx_out else w_in[l][:, OFF_K:OFF_HQ])
        fx = fourier_mix(col(ux, OFF_FOURIER, FOURIER_W), w_four[l])
        ax, ac = attention_group(ux, uc, base_c, q_norm[l], k_norm[l], tabs, ctx_out)
        rx, rc = hgrn_group(ux, uc, base_c, lb_all[:, l], hg_norm[l], ctx_out)
        x = x + g_a * (jnp.concatenate([fx, ax, rx], axis=-1) @ w_out[l])
        x = x + g_f * swiglu(rmsnorm_2(x) * (1 + sc_f) + sh_f, w_gate[l], w_up[l], w_down[l])
        if ctx_out:
            fc = fourier_mix(col(uc, OFF_FOURIER, FOURIER_W), w_four[l])
            ctx = ctx + mc[2] * (jnp.concatenate([fc, ac, rc], axis=-1) @ w_out[l])
            ctx = ctx + mc[5] * swiglu(rmsnorm_2(ctx) * (1 + mc[4]) + mc[3], w_gate[l], w_up[l], w_down[l])
    return rmsnorm_2(x, final_norm)


def setup_inputs(seed=0):
    out = dict(first_inputs(seed))
    for name, value in second_inputs(seed + 1).items():
        if name != "x":
            out[name + "_2"] = value
    return out


def reference(
    x, norm1_w, w_in, gla_w_a2, gla_b_a, gla_norm_w, w_out, norm2_w, w_ff1, w_ff2, rel_bias,
    final_norm_w, c_2, ctx_2, c_ctx_2, w_ada_2, b_ada_2, w_in_2, w_four_2, q_norm_2, k_norm_2,
    hg_lb_logits_2, hg_norm_2, w_out_2, w_gate_2, w_up_2, w_down_2, final_norm_2,
):
    x = first_block(
        x, norm1_w, w_in, gla_w_a2, gla_b_a, gla_norm_w, w_out, norm2_w, w_ff1, w_ff2, rel_bias,
        final_norm_w,
    )
    return second_block(
        x, c_2, ctx_2, c_ctx_2, w_ada_2, b_ada_2, w_in_2, w_four_2, q_norm_2, k_norm_2,
        hg_lb_logits_2, hg_norm_2, w_out_2, w_gate_2, w_up_2, w_down_2, final_norm_2,
    )


_drawn_inputs = setup_inputs


def setup_inputs(seed=0):
    import zlib

    import numpy as np

    out = dict(_drawn_inputs(seed))
    spreads = {}
    factors = {'norm1_w': 2.951,
     'gla_b_a': 3.081,
     'gla_norm_w': 6.65,
     'q_norm_2': 8.0,
     'k_norm_2': 8.0,
     'hg_norm_2': 7.691,
     'final_norm_2': 2.707}
    for name, (base, spread) in spreads.items():
        noise = np.random.default_rng([zlib.crc32(name.encode()), seed]).standard_normal(out[name].shape)
        drawn = base * np.exp(spread * noise) if base else spread * noise
        out[name] = __import__('jax').numpy.asarray(drawn.astype(out[name].dtype))
    for name, factor in factors.items():
        out[name] = (out[name] * factor).astype(out[name].dtype)
    return out
```

```python
import math
from contextlib import ExitStack

import numpy as np

import concourse.bass as bass
from concourse import mybir

F32 = mybir.dt.float32
F32R = mybir.dt.float32r
I32 = mybir.dt.int32
ALU = mybir.AluOpType
ACT = mybir.ActivationFunctionType
AX = mybir.AxisListType

P = 128
D = 1024
KT = D // P
SEQ = 512
CTX = 256
TOK = SEQ + CTX
NX = SEQ // P
NT = TOK // P
EPS = 1e-6
NEG = -1e30
PW = 256
HD = 64
A_W, B_QK, B_W, B_RANK, C_W = 384, 128, 256, 16, 384
IN_W = 3088
DFF1 = 4096
BUCKETS, MAX_DIST = 32, 2048
O_FOUR, O_Q, O_K, O_V, O_FF, O_FB, O_I, O_HQ, O_G = 0, 256, 768, 896, 1024, 1280, 1536, 1792, 2048
PROJ2 = 2304
DFF2 = 2816
LAYERS = 2
STRIP = 640
Z_FLOOR = -43.0
EXP_CAP = 85.0
SUB = 16

COLS = {}
for _name, _n in (("norm1", 8), ("norm2", 8), ("final1", 8), ("final2", 8), ("gla_b", 1), ("gla_norm", 2),
                  ("qn", 2), ("kn", 2), ("hgn", 2), ("lb", 8), ("b_ada", 96), ("c", 16)):
    COLS[_name] = (sum(n for _, n in COLS.values()), _n)
NCOLS = sum(n for _, n in COLS.values())


def w_panels():
    phases = {}

    def t_panel(w, col, cols, writer, tile, parts, row=0, kt=KT):
        return (w, row, kt, col, cols, [("T", m, writer, tile + m, parts) for m in range(cols // P)])

    def tok_panel(w, col, cols, out, tiles):
        return (w, 0, KT, col, cols, [("tok", t, "tok", out, None) for t in tiles])

    xs = range(NX)
    q = [t_panel("w_in", i * PW, PW, "proj", 2 * i, "x") for i in range(3)]
    q += [tok_panel("w_in", 768, 256, 0, xs), tok_panel("w_in", 1024, 128, 256, xs)]
    q += [t_panel("w_in", 1152, PW, "proj", 6, "x")]
    q += [tok_panel("w_in", 1408, 256, 384, xs)]
    q += [t_panel("w_in", 1664, PW, "proj", 8, "x")]
    q += [t_panel("w_in", 1920, P, "proj", 10, "x")]
    q += [t_panel("w_in", 1936 + i * PW, PW, "proj", 11 + 2 * i, "x") for i in range(3)]
    q += [tok_panel("w_in", 2704, 256, 640, xs), tok_panel("w_in", 2960, 128, 896, xs)]
    phases["in1"] = q
    phases["out1"] = [t_panel("w_out", i * PW, PW, "resid", 2 * i, "x") for i in range(4)]
    for g in range(4):
        phases[f"ff1_{g}"] = (
            [t_panel("w_ff1", g * D + i * PW, PW, "relu2", 2 * i, "x") for i in range(4)]
            + [t_panel("w_ff2", i * PW, PW, "resid", 2 * i, "x", row=g * D) for i in range(4)])
    for l in range(LAYERS):
        last = l == LAYERS - 1
        own = "x" if last else "xc"
        toks = range(NT)
        w = f"w_in2_{l}"
        q = [t_panel(w, O_FF, PW, "proj", 7, "xc"), t_panel(w, O_FB, PW, "proj", 9, "xc"),
             tok_panel(w, O_I, 256, 128, toks),
             t_panel(w, O_HQ, PW, "proj", 11, own), t_panel(w, O_G, PW, "proj", 13, own),
             t_panel(w, O_FOUR, PW, "proj", 0, own), t_panel(w, O_Q, PW, "proj", 2, own),
             t_panel(w, O_Q + PW, PW, "proj", 4, own), t_panel(w, O_K, P, "proj", 6, "xc"),
             tok_panel(w, O_V, 128, 0, toks)]
        phases[f"in2_{l}"] = q
        phases[f"out2_{l}"] = [t_panel(f"w_out2_{l}", i * PW, PW, "resid_a", 2 * i, own) for i in range(4)]
        t = DFF2 // P
        for g in range(3):
            kt = min(KT, t - KT * g)
            q = []
            for i in range(kt // 2):
                col = g * D + i * PW
                q += [t_panel(f"w_gate_{l}", col, PW, "gate", 2 * i, own),
                      t_panel(f"w_up_{l}", col, PW, "up", 2 * i, own)]
            q += [t_panel(f"w_down_{l}", i * PW, PW, "resid_f", 2 * i, own, row=g * D, kt=kt) for i in range(4)]
            phases[f"ff2_{l}_{g}"] = q
    return phases


def blocks_kernel(nc, dram, out_t):
    phases = w_panels()
    order = list(phases)
    ada = [("ada", l, i) for l in range(LAYERS) for i in range(6 * D // PW)]
    stream, where, n_ada = [], {}, 0
    for name in order:
        where[name] = []
        for panel in phases[name]:
            where[name].append(len(stream))
            stream.append(panel)
            if n_ada < len(ada):
                where[name].append(len(stream))
                stream.append(ada[n_ada])
                n_ada += 1
    mains = [i for i, s in enumerate(stream) if s[0] != "ada"]
    rank = {i: n for n, i in enumerate(mains)}
    ada_rank = {i: n for n, i in enumerate(i for i, s in enumerate(stream) if s[0] == "ada")}

    with ExitStack() as ctx:
        base = nc.sbuf_base + (-nc.sbuf_base) % 64
        at = [base]
        fence = ctx.enter_context(nc.sbuf_tensor("fence", [P, (nc.sbuf_usable_end - base) // 4 - 32], F32))
        del fence

        def put(name, shape, dt=F32, offset=None):
            size = 4 * math.prod(shape[1:])
            if offset is None:
                offset = at[0]
                at[0] += size + (-size) % 64
            assert offset + size <= nc.sbuf_usable_end, (name, offset, size)
            return nc.alloc_sbuf_tensor_at(name, shape, dt, offset=offset), offset

        class Signal:

            def __init__(self, handle, base=0, tally=None):
                self.sem, self.base, self.tally = handle, base, [0] if tally is None else tally

            def at(self, n):
                return self.base + n

            def up(self):
                self.tally[0] += 1
                return self.tally[0]

        def sem(name):
            return Signal(ctx.enter_context(nc.semaphore(name)))

        x, _ = put("x", [P, KT, SEQ])
        xc, xc_at = put("xc", [P, KT, CTX])
        raw, _ = put("raw", [P, 3, KT, PW])
        w_hi, _ = put("w_hi", [P, 2, KT, PW], F32R)
        w_lo, _ = put("w_lo", [P, 2, KT, PW], F32R)
        a_hi, hi_at = put("a_hi", [P, KT, TOK], F32R)
        a_lo, lo_at = put("a_lo", [P, KT, TOK], F32R)
        proj, proj_at = put("proj", [P, 17, TOK])
        tok_at = proj_at + 15 * TOK * 4
        tok2 = nc.alloc_sbuf_tensor_at("tok2", [P, NT, 384], F32, offset=tok_at)
        at[0] = proj_at + 54 * 1024
        proj1 = nc.alloc_sbuf_tensor_at("proj1", [P, 17, SEQ], F32, offset=proj_at)
        tok1 = nc.alloc_sbuf_tensor_at("tok1", [P, NX, 1024], F32, offset=proj_at + 17 * SEQ * 4)
        hid_hi = nc.alloc_sbuf_tensor_at("hid_hi", [P, KT, TOK], F32R, offset=proj_at)
        hid_lo = nc.alloc_sbuf_tensor_at("hid_lo", [P, KT, TOK], F32R, offset=proj_at + KT * TOK * 4)
        cols, _ = put("cols", [P, NCOLS])
        ident, _ = put("ident", [P, P])
        ones, _ = put("ones", [P, P])
        head_mean, _ = put("head_mean", [P, P])
        masks, _ = put("masks", [P, 2, 4, P], I32)
        reset, _ = put("reset", [P, TOK])
        mods, _ = put("mods", [P, LAYERS, 48, 2])
        silu_c, _ = put("silu_c", [P, KT, 2])
        small, _ = put("small", [P, 64])
        lbs, _ = put("lbs", [P, LAYERS, 2, 2, 2])
        zero, eps, one = small[:, 0:1], small[:, 1:2], small[:, 2:3]
        neg_m = small[:, 4:6]
        row_max = small[:, 6:8]
        row_sum = small[:, 8:10]
        row_inv = small[:, 10:12]
        total = small[:, 12:24]
        e_total = small[:, 24:36]
        s_at = at[0]
        assert s_at + 15 * 1024 <= nc.sbuf_usable_end, (s_at, nc.sbuf_usable_end)

        def over(name, shape, offset, dt=F32):
            assert offset + 4 * math.prod(shape[1:]) <= nc.sbuf_usable_end
            return nc.alloc_sbuf_tensor_at(name, shape, dt, offset=offset)

        K = 1024
        sq = over("sq", [P, 2, TOK], s_at)
        tmp = over("tmp", [P, 2, TOK], s_at + 6 * K)
        rstd = over("rstd", [P, TOK], s_at + 12 * K)
        prob = over("prob", [P, 2, TOK], s_at)
        prob_t = over("prob_t", [P, 2, NT, P], s_at + 6 * K)
        strips = over("strips", [P, 4, SEQ], xc_at)
        bias_row = over("bias_row", [12, STRIP], s_at)
        bias_add = over("bias_add", [12, STRIP], s_at + 3 * K)
        onehot = over("onehot", [BUCKETS, STRIP], s_at + 6 * K)
        rel = over("rel", [BUCKETS, 12], s_at + 9 * K)
        cum = over("cum", [P, 2 * TOK], s_at)
        dif = over("dif", [P, 2 * TOK], s_at + 6 * K)
        states = over("states", [P, NT, 2, HD], s_at + 12 * K)
        ev = over("ev", [P, 2 * TOK], hi_at)
        qe = over("qe", [P, 2 * TOK], hi_at + 6 * K)
        ke = over("ke", [P, 2 * TOK], hi_at + 12 * K)
        att = over("att", [P, 4 * TOK], lo_at)
        k_tok = over("k_tok", [P, NT, 2 * P], lo_at + 12 * K)
        w_a2 = over("w_a2", [B_RANK, B_QK], xc_at)
        f_tok = over("f_tok", [P, NT, 512], s_at)
        w_four = over("w_four", [P, 2, 256], s_at + 12 * K)
        f_feat = over("f_feat", [P, 256], s_at + 14 * K)
        f_tab = over("f_tab", [P, KT, SEQ], proj_at + 7 * TOK * 4)
        f_tab_c = over("f_tab_c", [P, 4, CTX], proj_at + 7 * TOK * 4 + 16 * K)
        f_z = over("f_z", [P, 2, TOK], hi_at + 6 * K)
        r_sq = over("r_sq", [P, 2, TOK], s_at)
        r_std = over("r_std", [P, TOK], s_at + 6 * K)
        r_tmp = over("r_tmp", [P, SEQ], s_at + 9 * K)
        r_cos = over("r_cos", [P, SEQ], s_at + 11 * K)
        r_sin = over("r_sin", [P, SEQ], s_at + 13 * K)
        turn = over("turn", [P, P], proj_at + 11 * TOK * 4)
        swap = over("swap", [P, P], proj_at + 11 * TOK * 4 + K)
        k_swap = over("k_swap", [P, TOK], proj_at + 7 * TOK * 4)

        PS = [ctx.enter_context(nc.psum_tensor(f"PS{i}", [P, 1024], F32)) for i in range(4)]
        bias_dram = nc.dram_tensor("bias_dram", [12, P, STRIP], F32)

        s_load = sem("constants_loaded")
        s_raw = [sem(f"raw_loaded{i}") for i in range(3)]
        s_hi = sem("w_hi_ready")
        s_lo = sem("w_lo_ready")
        s_ada = sem("ada_panel_used")
        s_adao = sem("ada_columns_out")
        s_acc = sem("tile_accumulated")
        s_fa = sem("tile_out_by_act")
        s_fd = sem("tile_out_by_dve")
        s_relu = sem("hidden_computed")
        s_hhi = sem("hidden_hi")
        s_setup = sem("setup_by_dve")
        s_setup_a = sem("setup_by_act")
        s_out = sem("output_stored")
        s_end = {e: sem(f"stage_end_{e}") for e in ("pe", "act", "dve")}
        a_step = sem("act_step")
        v_step = sem("dve_step")

        def col(name, i=0):
            o = COLS[name][0] + i
            return cols[:, o:o + 1]

        stage_of = {"pe": 0, "act": 0, "dve": 0}

        def stage_end(eng, name):
            stage_of[name] += 1
            eng.drain().then_inc(s_end[name].sem, 1)
            eng.wait_ge(s_end["pe"].sem, stage_of[name])
            eng.wait_ge(s_end["act"].sem, stage_of[name])
            eng.wait_ge(s_end["dve"].sem, stage_of[name])

        jobs = []
        for name in order:
            for i in where[name]:
                if stream[i][0] == "ada":
                    continue
                w, row, kt, c0, ncol, js = stream[i]
                for j in js:
                    jobs.append((i, j))
        ACT_WRITES = ("proj", "tok")
        job_of = {}
        n_act = n_dve = n_hid = n_silu = 0
        s_silu = sem("gate_activated")
        freed = []
        for n, (i, j) in enumerate(jobs):
            job_of.setdefault(i, []).append(n)
            if j[2] in ACT_WRITES:
                n_act += 1
                freed.append((s_fa, n_act))
            elif j[2] == "gate":
                n_silu += 1
                freed.append((s_silu, n_silu))
            elif j[2] in ("relu2", "up"):
                n_hid += 1
                freed.append((s_relu, n_hid))
            else:
                n_dve += 1
                freed.append((s_fd, n_dve))

        def slot(n):
            return PS[n % 4]

        def parts_of(parts):
            got = []
            if "x" in parts:
                got.append((x, slice(0, SEQ), slice(0, SEQ), 0))
            if "c" in parts:
                got.append((xc, slice(0, CTX), slice(SEQ, TOK), 1))
            return got

        def span(parts):
            return slice(0, TOK if "c" in parts else SEQ)

        block = ctx.enter_context(nc.Block())

        @block.sync
        def _(sp):
            for dst, name in ((x, "x"), (cols, "cols"), (ident, "ident"), (head_mean, "head_mean"), (masks, "masks"), (reset, "reset"), (bias_add, "bias_add"),
                              (onehot, "onehot"), (rel, "rel")):
                sp.dma_start(dst[:], dram[name]).then_inc(s_load.sem, 16)
            lo_done, ada_done = 0, 0
            for n, panel in enumerate(stream):
                if n >= 3:
                    if stream[n - 3][0] == "ada":
                        sp.wait_ge(s_ada.sem, ada_rank[n - 3] + 1)
                    else:
                        sp.wait_ge(s_lo.sem, rank[n - 3] + 1)
                if panel[0] == "ada":
                    _, l, i = panel
                    src = dram[f"w_ada_{l}"].rearrange("(k p) n -> p k n", p=P)[:, :, i * PW:(i + 1) * PW]
                    sp.dma_start(raw[:, n % 3], src).then_inc(s_raw[n % 3].sem, 16)
                else:
                    w, row, kt, c0, ncol, _ = panel
                    src = dram[w][row:row + kt * P, c0:c0 + ncol].rearrange("(k p) n -> p k n", p=P)
                    sp.dma_start(raw[:, n % 3, 0:kt, 0:ncol], src).then_inc(s_raw[n % 3].sem, 16)

        N_CONST = 9

        @block.gpsimd
        def _(pool):
            for i in mains:
                w, row, kt, c0, ncol, _ = stream[i]
                m = rank[i]
                pool.wait_ge(s_hi.sem, m + 1)
                src = raw[:, i % 3, 0:kt, 0:ncol]
                pool.tensor_tensor(w_lo[:, m % 2, 0:kt, 0:ncol], src, w_hi[:, m % 2, 0:kt, 0:ncol].bitcast(F32),
                                   ALU.subtract).then_inc(s_lo.sem, 1)

        stage_sems = {}

        def made(kind, i, name):
            if kind == "norm":
                return {"root": 1, "done": KT * (i in (2, 7)), "squared": KT, "summed": KT}.get(
                    name, KT * (i not in (2, 7)))
            if kind == "scan":
                return {"zps": i == 0, "z": i == 0, "e": i > 0, "f": i > 0, "dif": NL, "e_lv": NL, "factors": NL,
                        "scores": NL, "masked": NL, "in_out": 2, "turned": 1 + (i > 0), "k_tok": 1 + (i > 0)}.get(name, 1)
            if kind == "read":
                return {"means": 2, "root": 2}.get(name, 1)
            if kind == "att":
                groups, units = [att1, *att2][i]
                if name in ("low", "high"):
                    return len(groups)
                return 16 * 12 if name == "strip" else len(units)
            if kind == "four":
                nt = NX if i == LAYERS - 1 else NT
                return {"tables": 64, "feat": nt, "f_tok": nt}.get(name, 2)
            if kind == "rope":
                return {"tables": 64, "swapped": 1}.get(name, 5)

        def local(stage, name):
            kind, i = stage
            if (kind, name) not in stage_sems:
                stage_sems[kind, name] = sem(f"{kind}_{name}")
            shared = stage_sems[kind, name]
            return Signal(shared.sem, sum(int(made(kind, j, name)) for j in range(i)), shared.tally)


        def norm_plan(kind, l=0):
            if kind == "norm1":
                return "x", lambda k, c: (col("norm1", k), zero)
            if kind == "norm2":
                return "x", lambda k, c: (col("norm2", k), zero)
            own = "x" if l == LAYERS - 1 else "xc"
            if kind == "mod_a":
                return "xc", lambda k, c: (mods[:, l, 8 + k, c:c + 1], mods[:, l, k, c:c + 1])
            return own, lambda k, c: (mods[:, l, 32 + k, c:c + 1], mods[:, l, 24 + k, c:c + 1])

        def norm_act(a, st, parts, vec):
            sqd, summed, scaled, high = (local(st, s) for s in ("squared", "summed", "scaled", "high"))
            root = local(st, "root")
            for k in range(KT):
                if k - 1 > 0:
                    a.wait_ge(summed.sem, summed.at(k - 1))
                for n, (src, own, dst, c) in enumerate(parts_of(parts)):
                    end = n == len(parts) - 1
                    tell = sqd if end else a_step
                    nc.scalar.activation(sq[:, k % 2, dst], src[:, k, own], ACT.Square).then_inc(tell.sem, 1)
                    a.wait_ge(tell.sem, tell.up())
            a.wait_ge(summed.sem, summed.at(KT))
            sp_ = span(parts)
            nc.scalar.activation(rstd[:, sp_], PS[3][:, sp_], ACT.Sqrt, bias=eps, scale=1.0 / D).then_inc(root.sem, 1)
            a.wait_ge(root.sem, root.up())
            if vec is None:
                return
            for k in range(KT):
                a.wait_ge(scaled.sem, scaled.at(k + 1))
                for n, (src, own, dst, c) in enumerate(parts_of(parts)):
                    end = n == len(parts) - 1
                    tell = high if end else a_step
                    nc.scalar.activation(a_hi[:, k, dst], tmp[:, k % 2, dst], ACT.Identity, bias=vec(k, c)[1]).then_inc(tell.sem, 1)
                    a.wait_ge(tell.sem, tell.up())

        def norm_pe(p, st, parts):
            sqd, summed = local(st, "squared"), local(st, "summed")
            for k in range(KT):
                p.wait_ge(sqd.sem, sqd.at(k + 1))
                for src, own, dst, c in parts_of(parts):
                    mm = p.matmul(PS[3][:, dst], ones[:], sq[:, k % 2, dst], start=k == 0, stop=k == KT - 1)
                mm.then_inc(summed.sem, 1)

        def norm_dve(v, st, parts, vec):
            scaled, high, low = (local(st, s) for s in ("scaled", "high", "low"))
            root = local(st, "root")
            sp_ = span(parts)
            v.wait_ge(root.sem, root.at(1))
            nc.vector.reciprocal(rstd[:, sp_], rstd[:, sp_]).then_inc(v_step.sem, 1)
            v.wait_ge(v_step.sem, v_step.up())

            def lower(k):
                v.wait_ge(high.sem, high.at(k + 1))
                ps = parts_of(parts)
                for n, (src, own, dst, c) in enumerate(ps):
                    tell = low if n == len(ps) - 1 else v_step
                    nc.vector.scalar_tensor_tensor(a_lo[:, k, dst], tmp[:, k % 2, dst], vec(k, c)[1],
                                                        a_hi[:, k, dst].bitcast(F32), ALU.add, ALU.subtract).then_inc(tell.sem, 1)
                    v.wait_ge(tell.sem, tell.up())

            for k in range(KT):
                ps = parts_of(parts)
                for n, (src, own, dst, c) in enumerate(ps):
                    tell = scaled if n == len(ps) - 1 else v_step
                    nc.vector.scalar_tensor_tensor(tmp[:, k % 2, dst], src[:, k, own], vec(k, c)[0],
                                                        rstd[:, dst], ALU.mult, ALU.mult).then_inc(tell.sem, 1)
                    v.wait_ge(tell.sem, tell.up())
                if k:
                    lower(k - 1)
            lower(KT - 1)

        def final_dve(v, st, name, parts="x"):
            root, done = local(st, "root"), local(st, "done")
            v.wait_ge(root.sem, root.at(1))
            nc.vector.reciprocal(rstd[:, 0:SEQ], rstd[:, 0:SEQ]).then_inc(v_step.sem, 1)
            v.wait_ge(v_step.sem, v_step.up())
            for k in range(KT):
                nc.vector.scalar_tensor_tensor(x[:, k, :], x[:, k, :], col(name, k), rstd[:, 0:SEQ],
                                                    ALU.mult, ALU.mult).then_inc(done.sem, 1)
                v.wait_ge(done.sem, done.up())

        def operand(i):
            return (hid_hi, hid_lo) if stream[i][0].startswith(("w_ff2", "w_down")) else (a_hi, a_lo)

        hid_jobs = {}
        count = 0
        for i in mains:
            if any(j[2] in ("relu2", "up") for j in stream[i][5]):
                count += len(stream[i][5])
            hid_jobs[i] = count

        def gemm_pe(p, name):
            for i in where[name]:
                p.wait_ge(s_raw[i % 3].sem, 16 * (i // 3 + 1))
                if stream[i][0] == "ada":
                    gemm_pe_ada(p, i)
                    continue
                w, row, kt, c0, ncol, _ = stream[i]
                m = rank[i]
                hi, lo = w_hi[:, m % 2], w_lo[:, m % 2]
                b_hi, b_lo = operand(i)
                p.wait_ge(s_lo.sem, m + 1)
                if b_hi is hid_hi:
                    p.wait_ge(local(("hid", 0), "low").sem, local(("hid", 0), "low").at(hid_jobs[i]))
                for n in job_of[i]:
                    kind, idx, writer, tile, parts = jobs[n][1]
                    if n >= 4:
                        p.wait_ge(freed[n - 4][0].sem, freed[n - 4][1])
                    ps = slot(n)
                    for k in range(kt):
                        for t, (wv, av) in enumerate(((hi, b_hi), (hi, b_lo), (lo, b_hi))):
                            first, last = k == 0 and t == 0, k == kt - 1 and t == 2
                            if kind == "T":
                                for src, own, dst, c in parts_of(parts):
                                    mm = p.matmul(ps[:, dst], wv[:, k, idx * P:(idx + 1) * P], av[:, k, dst],
                                                  start=first, stop=last)
                            else:
                                mm = p.matmul(ps[:, 0:ncol], av[:, k, idx * P:(idx + 1) * P], wv[:, k, 0:ncol],
                                              start=first, stop=last)
                    mm.then_inc(s_acc.sem, 1)

        def gemm_pe_ada(p, i):
            n = ada_rank[i]
            if n >= 1:
                p.wait_ge(s_adao.sem, n)
            if n == 0:
                p.wait_ge(s_setup_a.sem, 1)
            ps = ada_ps(n)
            for m in range(PW // P):
                for k in range(KT):
                    mm = p.matmul(ps[:, 2 * m:2 * m + 2], raw[:, i % 3, k, m * P:(m + 1) * P], silu_c[:, k, :],
                                  start=k == 0, stop=k == KT - 1)
            mm.then_inc(s_ada.sem, 1)

        def ada_ps(n):
            return ADA_PS[:, 0:4]

        ADA_PS = PS[3][:, 1020:1024]

        def act_split(a, m):
            if m >= len(mains):
                return
            i = mains[m]
            w, row, kt, c0, ncol, _ = stream[i]
            a.wait_ge(s_raw[i % 3].sem, s_raw[i % 3].at(16 * (i // 3 + 1)))
            if m >= 2:
                if job_of[mains[m - 2]][-1] + 1 > 0:
                    a.wait_ge(s_acc.sem, s_acc.at(job_of[mains[m - 2]][-1] + 1))
            nc.scalar.activation(w_hi[:, m % 2, 0:kt, 0:ncol], raw[:, i % 3, 0:kt, 0:ncol], ACT.Copy).then_inc(s_hi.sem, 1)
            a.wait_ge(s_hi.sem, s_hi.up())

        def gemm_act(a, name):
            first_block = name == "in1"
            for i in where[name]:
                if stream[i][0] == "ada":
                    continue
                act_split(a, rank[i] + 1)
                ncol = stream[i][4]
                for n in job_of[i]:
                    kind, idx, writer, tile, parts = jobs[n][1]
                    ps = slot(n)
                    if writer in ("proj", "tok", "gate", "up"):
                        if writer != "up":
                            a.wait_ge(s_acc.sem, s_acc.at(n + 1))
                    if writer == "proj":
                        dst = (proj1 if first_block else proj)[:, tile, span(parts)]
                        scale = 1.0
                        if first_block and (tile < 3 or 11 <= tile < 14):
                            scale = HD ** -0.5
                        if first_block and tile == 6:
                            scale = 32 ** -0.5
                        nc.scalar.activation(dst, ps[:, span(parts)], ACT.Copy, scale=scale).then_inc(s_fa.sem, 1)
                        a.wait_ge(s_fa.sem, s_fa.up())
                    elif writer == "tok":
                        dst = (tok1 if first_block else tok2)[:, idx, tile:tile + ncol]
                        nc.scalar.activation(dst, ps[:, 0:ncol], ACT.Copy).then_inc(s_fa.sem, 1)
                        a.wait_ge(s_fa.sem, s_fa.up())
                    elif writer == "gate":
                        if hid_count(n) > 0:
                            a.wait_ge(s_relu.sem, s_relu.at(hid_count(n)))
                        nc.scalar.activation(sq[:, tile % 2, span(parts)], ps[:, span(parts)], ACT.Silu).then_inc(s_silu.sem, 1)
                        a.wait_ge(s_silu.sem, s_silu.up())
                    if writer in ("up", "relu2"):
                        h = hid_index[n]
                        a.wait_ge(s_relu.sem, s_relu.at(h + 1))
                        nc.scalar.activation(hid_hi[:, tile, span(parts)], tmp[:, h % 2, span(parts)], ACT.Copy).then_inc(s_hhi.sem, 1)
                        a.wait_ge(s_hhi.sem, s_hhi.up())

        hid_index = {}
        silu_index = {}
        for n, (i, j) in enumerate(jobs):
            if j[2] in ("relu2", "up"):
                hid_index[n] = len(hid_index)
            if j[2] == "gate":
                silu_index[n] = len(silu_index)
        relu_base = sum(1 for _, j in jobs if j[2] == "relu2")

        def hid_count(n):
            return relu_base + max(0, silu_index[n] - 1)

        def gemm_dve(v, name, l=0):
            for i in where[name]:
                if stream[i][0] == "ada":
                    n = ada_rank[i]
                    _, la, c = stream[i]
                    v.wait_ge(s_ada.sem, s_ada.at(n + 1))
                    o = COLS["b_ada"][0] + la * 48 + 2 * c
                    nc.vector.tensor_tensor(mods[:, la, 2 * c:2 * c + 2, :],
                                                 ADA_PS.rearrange("p (m c) -> p m c", c=2),
                                                 cols[:, o:o + 2].unsqueeze(2).to_broadcast([P, 2, 2]), ALU.add).then_inc(s_adao.sem, 1)
                    v.wait_ge(s_adao.sem, s_adao.up())
                    continue
                for n in job_of[i]:
                    kind, idx, writer, tile, parts = jobs[n][1]
                    if writer in ACT_WRITES or writer == "gate":
                        continue
                    v.wait_ge(s_acc.sem, s_acc.at(n + 1))
                    ps = slot(n)
                    pp = parts_of(parts)
                    sp_ = span(parts)
                    if writer.startswith("resid"):
                        for q, (dst, own, src, c) in enumerate(pp):
                            tell = s_fd if q == len(pp) - 1 else v_step
                            if writer == "resid":
                                nc.vector.tensor_tensor(dst[:, tile, own], ps[:, src], dst[:, tile, own], ALU.add).then_inc(tell.sem, 1)
                                v.wait_ge(tell.sem, tell.up())
                            else:
                                o = (16 if writer == "resid_a" else 40) + tile
                                nc.vector.scalar_tensor_tensor(dst[:, tile, own], ps[:, src], mods[:, l, o, c:c + 1],
                                                                    dst[:, tile, own], ALU.mult, ALU.add).then_inc(tell.sem, 1)
                                v.wait_ge(tell.sem, tell.up())
                        continue
                    h = hid_index[n]
                    low = local(("hid", 0), "low")
                    if writer == "relu2":
                        nc.vector.tensor_scalar(sq[:, 0, sp_], ps[:, sp_], 0.0, None, ALU.max).then_inc(v_step.sem, 1)
                        v.wait_ge(v_step.sem, v_step.up())
                        nc.vector.tensor_tensor(tmp[:, h % 2, sp_], sq[:, 0, sp_], sq[:, 0, sp_], ALU.mult).then_inc(s_relu.sem, 1)
                        v.wait_ge(s_relu.sem, s_relu.up())
                    else:
                        if silu_index[n - 2] + 1 > 0:
                            v.wait_ge(s_silu.sem, s_silu.at(silu_index[n - 2] + 1))
                        nc.vector.tensor_tensor(tmp[:, h % 2, sp_], ps[:, sp_], sq[:, tile % 2, sp_], ALU.mult).then_inc(s_relu.sem, 1)
                        v.wait_ge(s_relu.sem, s_relu.up())
                    v.wait_ge(s_hhi.sem, s_hhi.at(h + 1))
                    nc.vector.tensor_tensor(hid_lo[:, tile, sp_], tmp[:, h % 2, sp_],
                                                 hid_hi[:, tile, sp_].bitcast(F32), ALU.subtract).then_inc(low.sem, 1)
                    v.wait_ge(low.sem, low.up())

        def attention_plan(which, l=0):
            groups = []
            if which == "first":
                for half in range(2):
                    for pair in range(3):
                        units = []
                        for h in (2 * pair, 2 * pair + 1):
                            for i in range(NX):
                                qt, kt_ = (0, 3) if half == 0 else (11, 14)
                                units.append(dict(h=h, i=i, q=(proj1, qt + pair), k=(proj1, kt_ + pair),
                                                  rows=slice(HD * (h % 2), HD * (h % 2) + HD),
                                                  keys=(0, P * (i + 1)), strip=6 * half + h,
                                                  v=[tok1[:, t, (0 if half == 0 else 640) + HD * h:
                                                          (0 if half == 0 else 640) + HD * h + HD]
                                                     for t in range(i + 1)]))
                        groups.append(dict(units=units, tile=pair if half == 0 else 5 + pair, c0=0, n=SEQ))
            else:
                for part in range(1 if l == LAYERS - 1 else 2):
                    for pair in range(4):
                        units = []
                        for h in (2 * pair, 2 * pair + 1):
                            kv = h // 4
                            kt_ = (proj, 6) if h % 2 == kv else (k_swap, None)
                            key0, keyn = (0, TOK) if part == 0 else (SEQ, CTX)
                            for i in (range(NX) if part == 0 else range(NX, NT)):
                                units.append(dict(h=h, i=i, q=(proj, 2 + pair), k=kt_,
                                                  rows=slice(HD * (h % 2), HD * (h % 2) + HD),
                                                  keys=(key0, keyn), strip=None,
                                                  v=[tok2[:, key0 // P + t, HD * kv:HD * kv + HD]
                                                     for t in range(keyn // P)]))
                        groups.append(dict(units=units, tile=2 + pair, c0=0 if part == 0 else SEQ,
                                           n=SEQ if part == 0 else CTX))
            units = []
            for g, grp in enumerate(groups):
                for n, u in enumerate(grp["units"]):
                    u.update(group=g, first=n == 0, last=n == len(grp["units"]) - 1, c0=grp["c0"])
                    units.append(u)
            return groups, units

        def keys_ap(u):
            t, tile = u["k"]
            a, n = u["keys"]
            r = u["rows"]
            return lambda lo, hi: (t[r, tile, a + lo:a + hi] if tile is not None else t[r, a + lo:a + hi])

        def att_pe(p, st, groups, units):
            S = lambda n: local(st, n)
            N = len(units)
            for s in range(N + 2):
                if s < N:
                    u = units[s]
                    if s >= 2:
                        if s - 1 > 0:
                            p.wait_ge(S("exp").sem, S("exp").at(s - 1))
                    q = u["q"][0][u["rows"], u["q"][1], u["i"] * P:(u["i"] + 1) * P]
                    k = keys_ap(u)
                    n = u["keys"][1]
                    for lo in range(0, n, 512):
                        hi = min(n, lo + 512)
                        mm = p.matmul(PS[s % 2][:, lo:hi], q, k(lo, hi), start=True, stop=True)
                    mm.then_inc(S("scores").sem, 1)
                if 1 <= s <= N:
                    t = s - 1
                    p.wait_ge(S("norm").sem, S("norm").at(t + 1))
                    if t:
                        if t > 0:
                            p.wait_ge(S("copied").sem, S("copied").at(t))
                    nb = units[t]["keys"][1] // P
                    for b in range(nb):
                        mm = p.transpose(PS[2][:, b * P:(b + 1) * P], prob[:, t % 2, b * P:(b + 1) * P], ident[:])
                    mm.then_inc(S("turned").sem, 1)
                if s >= 2:
                    t = s - 2
                    u = units[t]
                    p.wait_ge(S("copied").sem, S("copied").at(t + 1))
                    if u["first"] and u["group"] >= 2:
                        if u["group"] - 1 > 0:
                            p.wait_ge(S("low").sem, S("low").at(u["group"] - 1))
                    o = 512 * (u["group"] % 2) + u["i"] * P - u["c0"]
                    for b, vv in enumerate(u["v"]):
                        mm = p.matmul(PS[3][u["rows"], o:o + P], vv, prob_t[:, t % 2, b, :],
                                      start=b == 0, stop=b == len(u["v"]) - 1)
                    mm.then_inc(S("values").sem, 1)

        def att_dve(v, st, groups, units):
            S = lambda n: local(st, n)
            N = len(units)
            for s in range(N + 4):
                if 1 <= s <= N:
                    t = s - 1
                    n = units[t]["keys"][1]
                    v.wait_ge(S("exp").sem, S("exp").at(t + 1))
                    nc.vector.reciprocal(row_inv[:, t % 2:t % 2 + 1], row_sum[:, t % 2:t % 2 + 1]).then_inc(v_step.sem, 1)
                    v.wait_ge(v_step.sem, v_step.up())
                    nc.vector.tensor_scalar(prob[:, t % 2, 0:n], prob[:, t % 2, 0:n], row_inv[:, t % 2:t % 2 + 1],
                                                 None, ALU.mult).then_inc(S("norm").sem, 1)
                    v.wait_ge(S("norm").sem, S("norm").up())
                if s < N:
                    u = units[s]
                    v.wait_ge(S("scores").sem, S("scores").at(s + 1))
                    n = u["keys"][1]
                    if u["strip"] is not None:
                        head = u["strip"]
                        v.wait_ge(S("strip").sem, S("strip").at(16 * max(3, head + 1)))
                        if s - 1 > 0:
                            v.wait_ge(S("turned").sem, S("turned").at(s - 1))
                        nc.vector.tensor_tensor_reduce(prob[:, s % 2, 0:n], PS[s % 2][:, 0:n],
                                                            strips[:, head % 4, SEQ - n:SEQ], 1.0, NEG, ALU.add, ALU.max,
                                                            row_max[:, s % 2:s % 2 + 1]).then_inc(S("biased").sem, 1)
                        v.wait_ge(S("biased").sem, S("biased").up())
                        nc.vector.tensor_scalar(neg_m[:, s % 2:s % 2 + 1], row_max[:, s % 2:s % 2 + 1], -1.0, None,
                                                     ALU.mult).then_inc(S("max").sem, 1)
                        v.wait_ge(S("max").sem, S("max").up())
                    else:
                        nc.vector.tensor_reduce(neg_m[:, s % 2:s % 2 + 1], PS[s % 2][:, 0:n], AX.X, ALU.max,
                                                     negate=True).then_inc(S("max").sem, 1)
                        v.wait_ge(S("max").sem, S("max").up())
                if 3 <= s <= N + 2 and units[s - 3]["last"]:
                    g = units[s - 3]["group"]
                    grp = groups[g]
                    v.wait_ge(S("high").sem, S("high").at(g + 1))
                    c = slice(grp["c0"], grp["c0"] + grp["n"])
                    o = 512 * (g % 2)
                    nc.vector.tensor_tensor(a_lo[:, grp["tile"], c], PS[3][:, o:o + grp["n"]],
                                                 a_hi[:, grp["tile"], c].bitcast(F32), ALU.subtract).then_inc(S("low").sem, 1)
                    v.wait_ge(S("low").sem, S("low").up())

        def att_act(a, st, groups, units):
            S = lambda n: local(st, n)
            N = len(units)
            if units[0]["strip"] is not None:
                def strip(head):
                    src = bass.AP(bias_dram, head * P * STRIP + P - 1, [[STRIP - 1, P], [1, SEQ]])
                    a.dma_start(strips[:, head % 4, :], src).then_inc(S("strip").sem, 16)
                a.wait_ge(s_load_bias.sem, s_load_bias.at(16))
                for head in range(3):
                    strip(head)
            for s in range(N + 4):
                if 1 <= s <= N:
                    t = s - 1
                    a.wait_ge(S("turned").sem, S("turned").at(t + 1))
                    if t - 1 > 0:
                        a.wait_ge(S("values").sem, S("values").at(t - 1))
                    nb = units[t]["keys"][1] // P
                    nc.scalar.activation(prob_t[:, t % 2, 0:nb, :].rearrange("p b q -> p (b q)"),
                                              PS[2][:, 0:nb * P], ACT.Copy).then_inc(S("copied").sem, 1)
                    a.wait_ge(S("copied").sem, S("copied").up())
                if s < N:
                    u = units[s]
                    n = u["keys"][1]
                    if u["strip"] is not None and s % NX == 0 and 1 <= s // NX and s // NX + 2 < 12:
                        a.wait_ge(S("biased").sem, S("biased").at(s))
                        a.wait_ge(S("strip").sem, S("strip").at(16 * (s // NX + 2)))
                        strip(s // NX + 2)
                    a.wait_ge(S("max").sem, S("max").at(s + 1))
                    if u["strip"] is None:
                        if s - 1 > 0:
                            a.wait_ge(S("turned").sem, S("turned").at(s - 1))
                    src = prob[:, s % 2, 0:n] if u["strip"] is not None else PS[s % 2][:, 0:n]
                    nc.scalar.activation(prob[:, s % 2, 0:n], src, ACT.Exp, bias=neg_m[:, s % 2:s % 2 + 1],
                                              accum_out=row_sum[:, s % 2:s % 2 + 1]).then_inc(S("exp").sem, 1)
                    a.wait_ge(S("exp").sem, S("exp").up())
                if 3 <= s <= N + 2 and units[s - 3]["last"]:
                    g = units[s - 3]["group"]
                    grp = groups[g]
                    if s - 2 > 0:
                        a.wait_ge(S("values").sem, S("values").at(s - 2))
                    c = slice(grp["c0"], grp["c0"] + grp["n"])
                    o = 512 * (g % 2)
                    nc.scalar.activation(a_hi[:, grp["tile"], c], PS[3][:, o:o + grp["n"]], ACT.Copy).then_inc(S("high").sem, 1)
                    a.wait_ge(S("high").sem, S("high").up())

        s_load_bias = sem("bias_rows_stored")

        class Scan:

            def __init__(self, kind, back=False, l=0):
                self.back = back
                self.gla = kind == "gla"
                self.dk = 32 if self.gla else HD
                self.H = 1 if self.gla else 2
                self.T = SEQ if self.gla else TOK
                self.n_out = NX if self.gla or l == LAYERS - 1 else NT
                fwd = list(range(NX)) if self.gla else [4, 5, 0, 1, 2, 3]
                self.tiles = fwd if not back else [5, 4, 3, 2, 1, 0]
                self.l = l
                if self.gla:
                    self.q = proj1[:, 6:7, 0:SEQ]
                    self.k = proj1[:, 7:8, 0:SEQ]
                    self.v = lambda t, h: tok1[:, t, 384 + HD * h:384 + HD * h + HD]
                else:
                    z = 9 if back else 7
                    self.q = proj[:, 11:13, :]
                    self.k = proj[:, z:z + 2, :]
                    self.v = lambda t, h: tok2[:, t, P + HD * h:P + HD * h + HD]
                self.own = P * self.n_out

            def view(self, t, n=None):
                n = self.T if n is None else n
                return t[:, 0:self.H * self.T].rearrange("p (h t) -> p h t", h=self.H)[:, :, 0:n]

            def rows(self, h):
                return slice(self.dk * h, self.dk * h + self.dk) if self.gla else slice(HD * (h % 2), HD * (h % 2) + HD)

            def half(self, h):
                return 0 if self.gla else h // 2

        NL = 4

        def gates_dve(v, st, s):
            S = lambda n: local(st, n)
            if s.gla:
                z, e = s.view(cum), s.view(ev)
                d = s.view(dif)
                v.wait_ge(S("z").sem, S("z").at(1))
                nc.vector.scalar_tensor_tensor(e, z, -1.0, z, ALU.mult, ALU.max).then_inc(S("prep").sem, 1)
                v.wait_ge(S("prep").sem, S("prep").up())
                v.wait_ge(S("ln").sem, S("ln").at(1))
                nc.vector.scalar_tensor_tensor(d, z, 0.0, e, ALU.min, ALU.subtract).then_inc(v_step.sem, 1)
                v.wait_ge(v_step.sem, v_step.up())
                nc.vector.tensor_scalar(d, d, 1.0 / 16.0, None, ALU.mult).then_inc(v_step.sem, 1)
                v.wait_ge(v_step.sem, v_step.up())
                lf = dif
            else:
                z, e, f = s.k, s.view(ev), s.view(dif)
                b = int(s.back)
                nc.vector.tensor_scalar(z, z, Z_FLOOR, None, ALU.max).then_inc(S("prep").sem, 1)
                v.wait_ge(S("prep").sem, S("prep").up())
                v.wait_ge(S("e").sem, S("e").at(1))
                nc.vector.tensor_scalar(f, e, 1.0, None, ALU.add).then_inc(v_step.sem, 1)
                v.wait_ge(v_step.sem, v_step.up())
                nc.vector.reciprocal(f, f).then_inc(v_step.sem, 1)
                v.wait_ge(v_step.sem, v_step.up())
                for h in range(2):
                    lb, oml = lbs[:, s.l, b, h, 0:1], lbs[:, s.l, b, h, 1:2]
                    nc.vector.scalar_tensor_tensor(z[:, h, :], e[:, h, :], oml, f[:, h, :], ALU.mult, ALU.mult).then_inc(v_step.sem, 1)
                    v.wait_ge(v_step.sem, v_step.up())
                    tell = S("f") if h == 1 else v_step
                    nc.vector.tensor_scalar(f[:, h, :], f[:, h, :], oml, lb, ALU.mult, ALU.add).then_inc(tell.sem, 1)
                    v.wait_ge(tell.sem, tell.up())
                v.wait_ge(S("ln").sem, S("ln").at(1))
                lf = ev
            for h in range(s.H):
                nc.vector.tensor_tensor_scan(cum[:, h * s.T:(h + 1) * s.T], reset[:, 0:s.T],
                                                  lf[:, h * s.T:(h + 1) * s.T], 0.0, ALU.mult, ALU.add).then_inc(v_step.sem, 1)
                v.wait_ge(v_step.sem, v_step.up())
            tv = total[:, 0:s.H * s.T // P].rearrange("p (h t) -> p h t", h=s.H)
            nc.vector.tensor_copy(tv, s.view(cum).rearrange("p h (t c) -> p h t c", c=P)[:, :, :, P - 1]).then_inc(S("total").sem, 1)
            v.wait_ge(S("total").sem, S("total").up())
            if s.back:
                nc.vector.tensor_tensor(s.view(cum), s.view(cum), s.view(lf), ALU.subtract).then_inc(v_step.sem, 1)
                v.wait_ge(v_step.sem, v_step.up())

        def gates_act(a, st, s):
            S = lambda n: local(st, n)
            if s.gla:
                a.wait_ge(S("zps").sem, S("zps").at(1))
                nc.scalar.activation(cum[:, 0:SEQ], PS[0][:, 0:SEQ], ACT.Identity, bias=col("gla_b")).then_inc(S("z").sem, 1)
                a.wait_ge(S("z").sem, S("z").up())
                a.wait_ge(S("prep").sem, S("prep").at(1))
                nc.scalar.activation(s.view(ev), s.view(ev), ACT.Exp, scale=-1.0).then_inc(a_step.sem, 1)
                a.wait_ge(a_step.sem, a_step.up())
                nc.scalar.activation(s.view(ev), s.view(ev), ACT.Ln, bias=one).then_inc(S("ln").sem, 1)
                a.wait_ge(S("ln").sem, S("ln").up())
            else:
                a.wait_ge(S("prep").sem, S("prep").at(1))
                nc.scalar.activation(s.view(ev), s.k, ACT.Exp, scale=-1.0).then_inc(S("e").sem, 1)
                a.wait_ge(S("e").sem, S("e").up())
                a.wait_ge(S("f").sem, S("f").at(1))
                nc.scalar.activation(s.view(ev), s.view(dif), ACT.Ln).then_inc(S("ln").sem, 1)
                a.wait_ge(S("ln").sem, S("ln").up())
            a.wait_ge(S("total").sem, S("total").at(1))
            n = s.H * s.T // P
            nc.scalar.activation(e_total[:, 0:n], total[:, 0:n], ACT.Exp).then_inc(S("e_total").sem, 1)
            a.wait_ge(S("e_total").sem, S("e_total").up())

        def gates_pe(p, st, s):
            if s.gla:
                p.wait_ge(s_wa2.sem, 16)
                p.matmul(PS[0][:, 0:SEQ], w_a2[:], proj1[0:B_RANK, 10, :], start=True, stop=True).then_inc(local(st, "zps").sem, 1)

        s_wa2 = sem("w_a2_loaded")

        def levels_dve(v, st, s):
            S = lambda n: local(st, n)
            n = s.H * s.T
            n_own = s.own
            nc.vector.memset(att[:, 0:4 * n_own], 0.0).then_inc(v_step.sem, 1)
            v.wait_ge(v_step.sem, v_step.up())
            def differences(lv):
                if lv < 3:
                    bs = 64 >> lv
                    c = cum[:, 0:n].rearrange("p (g two b) -> p g two b", two=2, b=bs)
                    d = dif[:, 0:n].rearrange("p (g two b) -> p g two b", two=2, b=bs)
                    ref = c[:, :, 0, bs - 1:bs].to_broadcast([P, n // (2 * bs), bs])
                    if s.back:
                        ref = c[:, :, 1, 0:1].to_broadcast([P, n // (2 * bs), bs])
                    nc.vector.tensor_tensor(d[:, :, 0, :], ref, c[:, :, 0, :], ALU.subtract).then_inc(v_step.sem, 1)
                    v.wait_ge(v_step.sem, v_step.up())
                    nc.vector.tensor_tensor(d[:, :, 1, :], c[:, :, 1, :], ref, ALU.subtract).then_inc(S("dif").sem, 1)
                    v.wait_ge(S("dif").sem, S("dif").up())
                else:
                    c = cum[:, 0:n].rearrange("p (g b) -> p g b", b=SUB)
                    d = dif[:, 0:n].rearrange("p (g b) -> p g b", b=SUB)
                    mid = c[:, :, SUB // 2:SUB // 2 + 1].to_broadcast([P, n // SUB, SUB])
                    nc.vector.tensor_tensor(d, c, mid, ALU.subtract).then_inc(v_step.sem, 1)
                    v.wait_ge(v_step.sem, v_step.up())
                    nc.vector.tensor_scalar(dif[:, 0:n], dif[:, 0:n], -EXP_CAP, EXP_CAP, ALU.max, ALU.min).then_inc(S("dif").sem, 1)
                    v.wait_ge(S("dif").sem, S("dif").up())

            differences(0)
            for lv in range(NL):
                if lv > 0:
                    v.wait_ge(S("scores").sem, S("scores").at(lv))
                v.wait_ge(S("e_lv").sem, S("e_lv").at(lv + 1))
                nc.vector.tensor_tensor(s.view(qe, n_own), s.q[:, :, 0:n_own], s.view(ev, n_own), ALU.mult).then_inc(v_step.sem, 1)
                v.wait_ge(v_step.sem, v_step.up())
                if lv < 3:
                    nc.vector.tensor_tensor(s.view(ke, n_own), s.k[:, :, 0:n_own], s.view(ev, n_own), ALU.mult).then_inc(S("factors").sem, 1)
                    v.wait_ge(S("factors").sem, S("factors").up())
                else:
                    v.wait_ge(S("e_neg").sem, S("e_neg").at(1))
                    nc.vector.tensor_tensor(s.view(ke, n_own), s.k[:, :, 0:n_own], s.view(dif, n_own), ALU.mult).then_inc(S("factors").sem, 1)
                    v.wait_ge(S("factors").sem, S("factors").up())
                if lv < NL - 1:
                    v.wait_ge(S("e_lv").sem, S("e_lv").at(lv + 1))
                    differences(lv + 1)
                v.wait_ge(S("scores").sem, S("scores").at(lv + 1))
                m = masks[:, int(s.back), lv, :]
                for part in range(3 if s.n_out > NX else 2):
                    o, w = (1024 * part, 1024)
                    tell = S("masked") if part == (2 if s.n_out > NX else 1) else v_step
                    nc.vector.copy_predicated(att[:, o:o + w].rearrange("p (g t) -> p g t", t=P),
                                                   m.unsqueeze(1).to_broadcast([P, w // P, P]),
                                                   PS[part][:, 0:w].rearrange("p (g t) -> p g t", t=P)).then_inc(tell.sem, 1)
                    v.wait_ge(tell.sem, tell.up())

        def att_col(s, h, t):
            return (h * NX + t) * P if t < NX else 4 * SEQ + ((h % 2 * 2 + h // 2) * 2 + t - NX) * P

        def levels_act(a, st, s):
            S = lambda n: local(st, n)
            n = s.H * s.T
            for lv in range(NL):
                a.wait_ge(S("dif").sem, S("dif").at(lv + 1))
                if lv > 0:
                    a.wait_ge(S("factors").sem, S("factors").at(lv))
                sign = -1.0 if (lv == 3 and s.back) else 1.0
                nc.scalar.activation(ev[:, 0:n], dif[:, 0:n], ACT.Exp, scale=sign).then_inc(S("e_lv").sem, 1)
                a.wait_ge(S("e_lv").sem, S("e_lv").up())
                if lv == 3:
                    nc.scalar.activation(dif[:, 0:n], dif[:, 0:n], ACT.Exp, scale=-sign).then_inc(S("e_neg").sem, 1)
                    a.wait_ge(S("e_neg").sem, S("e_neg").up())

        def levels_pe(p, st, s):
            S = lambda n: local(st, n)
            q, k = s.view(qe), s.view(ke)
            for lv in range(NL):
                p.wait_ge(S("factors").sem, S("factors").at(lv + 1))
                if lv:
                    if lv > 0:
                        p.wait_ge(S("masked").sem, S("masked").at(lv))
                for h in range(4):
                    for t in range(s.n_out):
                        o = att_col(s, h, t)
                        ts = slice(t * P, (t + 1) * P)
                        mm = p.matmul(PS[o // 1024][:, o % 1024:o % 1024 + P], k[s.rows(h), s.half(h), ts],
                                      q[s.rows(h), s.half(h), ts], start=True, stop=True)
                mm.then_inc(S("scores").sem, 1)

        def state_dve(v, st, s):
            S = lambda n: local(st, n)
            nt = s.T // P
            c = s.view(cum).rearrange("p h (t c) -> p h t c", c=P)
            d = s.view(dif).rearrange("p h (t c) -> p h t c", c=P)
            tv = total[:, 0:s.H * nt].rearrange("p (h t) -> p h t", h=s.H)
            for h in range(s.H):
                tell = S("rest") if h == s.H - 1 else v_step
                nc.vector.tensor_tensor(d[:, h], tv[:, h].unsqueeze(2).to_broadcast([P, nt, P]), c[:, h],
                                             ALU.subtract).then_inc(tell.sem, 1)
                v.wait_ge(tell.sem, tell.up())
            v.wait_ge(S("in_out").sem, S("in_out").at(2))
            into, outof = (s.view(ev), s.view(dif)) if not s.back else (s.view(dif), s.view(ev))
            n_own = s.own
            nc.vector.tensor_tensor(s.view(qe, n_own), s.q[:, :, 0:n_own], into[:, :, 0:n_own], ALU.mult).then_inc(v_step.sem, 1)
            v.wait_ge(v_step.sem, v_step.up())
            nc.vector.tensor_tensor(s.view(ke), s.k, outof, ALU.mult).then_inc(S("outgoing").sem, 1)
            v.wait_ge(S("outgoing").sem, S("outgoing").up())
            v.wait_ge(S("e_total").sem, S("e_total").at(1))
            first = s.tiles[0]
            nc.vector.memset(states[:, first], 0.0).then_inc(v_step.sem, 1)
            v.wait_ge(v_step.sem, v_step.up())
            v.wait_ge(S("updates").sem, S("updates").at(1))
            for a_, b_ in zip(s.tiles, s.tiles[1:]):
                for h in range(s.H):
                    u = PS[3][:, a_ * P + h * HD:a_ * P + h * HD + HD]
                    tell = S("states") if (b_ == s.tiles[-1] and h == s.H - 1) else v_step
                    nc.vector.scalar_tensor_tensor(states[:, b_, h, :], states[:, a_, h, :],
                                                        e_total[:, h * nt + a_:h * nt + a_ + 1], u, ALU.mult, ALU.add).then_inc(tell.sem, 1)
                    v.wait_ge(tell.sem, tell.up())

        def state_act(a, st, s):
            S = lambda n: local(st, n)
            n = s.H * s.T
            a.wait_ge(S("factors").sem, S("factors").at(NL))
            nc.scalar.activation(ev[:, 0:n], cum[:, 0:n], ACT.Exp).then_inc(S("in_out").sem, 1)
            a.wait_ge(S("in_out").sem, S("in_out").up())
            a.wait_ge(S("rest").sem, S("rest").at(1))
            nc.scalar.activation(dif[:, 0:n], dif[:, 0:n], ACT.Exp).then_inc(S("in_out").sem, 1)
            a.wait_ge(S("in_out").sem, S("in_out").up())
            w = s.H * P
            for r, ts in enumerate([range(0, 4), range(4, s.T // P)][:1 if s.gla else 2]):
                a.wait_ge(S("turned").sem, S("turned").at(r + 1))
                m = len(ts)
                nc.scalar.activation(k_tok[:, ts[0]:ts[-1] + 1, 0:w],
                                          PS[r][:, 0:m * w].rearrange("p (t c) -> p t c", c=w), ACT.Copy).then_inc(S("k_tok").sem, 1)
                a.wait_ge(S("k_tok").sem, S("k_tok").up())

        def state_pe(p, st, s):
            S = lambda n: local(st, n)
            p.wait_ge(S("outgoing").sem, S("outgoing").at(1))
            p.wait_ge(S("masked").sem, S("masked").at(NL))
            k = s.view(ke)
            w = s.H * P
            rounds = [range(0, 4), range(4, s.T // P)][:1 if s.gla else 2]
            for r, ts in enumerate(rounds):
                for t in ts:
                    for h in range(s.H):
                        o = (t - ts[0]) * w + h * P
                        mm = p.transpose(PS[r][:, o:o + P], k[:, h, t * P:(t + 1) * P], ident[:])
                mm.then_inc(S("turned").sem, 1)
            if len(rounds) > 0:
                p.wait_ge(S("k_tok").sem, S("k_tok").at(len(rounds)))
            for t in range(s.T // P):
                for h in range(4):
                    o = t * P + s.half(h) * HD
                    c = s.dk * h if s.gla else HD * h
                    mm = p.matmul(PS[3][s.rows(h), o:o + HD], k_tok[:, t, c:c + s.dk], s.v(t, h), start=True, stop=True)
            mm.then_inc(S("updates").sem, 1)
            p.wait_ge(S("states").sem, S("states").at(1))
            for h in range(4):
                for t in range(s.n_out):
                    rows = slice(HD * (h % 2), HD * (h % 2) + HD)
                    o = t * P
                    dst = PS[h // 2][rows, o:o + P]
                    a_ = att_col(s, h, t)
                    p.matmul(dst, s.v(t, h), att[:, a_:a_ + P], start=True, stop=False)
                    mm = p.matmul(dst, states[s.rows(h), t, s.half(h), :],
                                  s.view(qe)[s.rows(h), s.half(h), t * P:(t + 1) * P], start=False, stop=True)
            mm.then_inc(S("outputs").sem, 1)

        def scan_out_dve(v, st, s, dst, add):
            S = lambda n: local(st, n)
            v.wait_ge(S("outputs").sem, S("outputs").at(1))
            for h in range(2):
                if add:
                    nc.vector.tensor_tensor(dst[:, h, 0:s.own], PS[h][:, 0:s.own], dst[:, h, 0:s.own], ALU.add).then_inc(v_step.sem, 1)
                    v.wait_ge(v_step.sem, v_step.up())
                else:
                    nc.vector.tensor_copy(dst[:, h, 0:s.own], PS[h][:, 0:s.own]).then_inc(v_step.sem, 1)
                    v.wait_ge(v_step.sem, v_step.up())

        def read_act(a, st, o, g, n, tile):
            S = lambda n_: local(st, n_)
            w = s_view(ev, n)
            nc.scalar.activation(w, o, ACT.Square).then_inc(S("squared").sem, 1)
            a.wait_ge(S("squared").sem, S("squared").up())
            for h in range(2):
                a.wait_ge(S("means").sem, S("means").at(h + 1))
                nc.scalar.activation(s_view(dif, n)[:, h, :], PS[h][:, 0:n], ACT.Sqrt, bias=eps).then_inc(S("root").sem, 1)
                a.wait_ge(S("root").sem, S("root").up())
            nc.scalar.activation(s_view(qe, n), g, ACT.Silu).then_inc(S("silu").sem, 1)
            a.wait_ge(S("silu").sem, S("silu").up())
            a.wait_ge(S("product").sem, S("product").at(1))
            nc.scalar.activation(a_hi[:, tile:tile + 2, 0:n], s_view(cum, n), ACT.Copy).then_inc(S("high").sem, 1)
            a.wait_ge(S("high").sem, S("high").up())

        def s_view(t, n):
            return t[:, 0:2 * n].rearrange("p (h t) -> p h t", h=2)

        def read_pe(p, st, n):
            S = lambda n_: local(st, n_)
            p.wait_ge(S("squared").sem, S("squared").at(1))
            for h in range(2):
                for lo in range(0, n, 512):
                    hi = min(n, lo + 512)
                    mm = p.matmul(PS[h][:, lo:hi], head_mean[:], s_view(ev, n)[:, h, lo:hi], start=True, stop=True)
                mm.then_inc(S("means").sem, 1)

        def read_dve(v, st, o, gain, n, tile):
            S = lambda n_: local(st, n_)
            v.wait_ge(S("root").sem, S("root").at(2))
            r = s_view(dif, n)
            nc.vector.reciprocal(r, r).then_inc(v_step.sem, 1)
            v.wait_ge(v_step.sem, v_step.up())
            for h in range(2):
                nc.vector.scalar_tensor_tensor(r[:, h, :], o[:, h, :], gain(h), r[:, h, :], ALU.mult, ALU.mult).then_inc(v_step.sem, 1)
                v.wait_ge(v_step.sem, v_step.up())
            v.wait_ge(S("silu").sem, S("silu").at(1))
            nc.vector.tensor_tensor(s_view(cum, n), r, s_view(qe, n), ALU.mult).then_inc(S("product").sem, 1)
            v.wait_ge(S("product").sem, S("product").up())
            v.wait_ge(S("high").sem, S("high").at(1))
            nc.vector.tensor_tensor(a_lo[:, tile:tile + 2, 0:n], s_view(cum, n),
                                         a_hi[:, tile:tile + 2, 0:n].bitcast(F32), ALU.subtract).then_inc(v_step.sem, 1)
            v.wait_ge(v_step.sem, v_step.up())

        def four_pe(p, st, l):
            S = lambda n: local(st, n)
            nt = NX if l == LAYERS - 1 else NT
            p.wait_ge(S("tables").sem, S("tables").at(64))
            for t in range(nt):
                if t >= 2:
                    if t - 1 > 0:
                        p.wait_ge(S("f_tok").sem, S("f_tok").at(t - 1))
                for h in range(2):
                    mm = p.matmul(PS[t % 2][:, h * 256:(h + 1) * 256], proj[:, h, t * P:(t + 1) * P], f_feat[:],
                                  start=True, stop=True)
                mm.then_inc(S("feat").sem, 1)
            p.wait_ge(S("f_tok").sem, S("f_tok").at(nt))
            for h in range(2):
                for c in range(2):
                    for t in range(NX):
                        mm = p.matmul(PS[2 + h][:, 0:SEQ], f_tok[:, t, 256 * h + P * c:256 * h + P * c + P],
                                      f_tab[:, 4 * c + t, :], start=c == 0 and t == 0, stop=c == 1 and t == NX - 1)
                if nt > NX:
                    for c in range(2):
                        for t in range(2):
                            mm = p.matmul(PS[2 + h][:, SEQ:TOK], f_tok[:, NX + t, 256 * h + P * c:256 * h + P * c + P],
                                          f_tab_c[:, 2 * c + t, :], start=c == 0 and t == 0, stop=c == 1 and t == 1)
                mm.then_inc(S("z").sem, 1)
            p.wait_ge(S("f_z").sem, S("f_z").at(2))
            n = nt * P
            for m in range(2):
                for lo in range(0, n, 512):
                    hi = min(n, lo + 512)
                    for h in range(2):
                        mm = p.matmul(PS[m][:, lo:hi], w_four[:, h, m * P:(m + 1) * P], f_z[:, h, lo:hi],
                                      start=h == 0, stop=h == 1)
                mm.then_inc(S("mixed").sem, 1)

        def four_act(a, st, l):
            S = lambda n: local(st, n)
            nt = NX if l == LAYERS - 1 else NT
            n = nt * P
            for dst, src in ((f_feat[:], dram["f_feat"]), (f_tab[:], dram["f_tab"]), (f_tab_c[:], dram["f_tab_c"]),
                             (w_four[:], dram[f"w_four_{l}"].rearrange("(h p) n -> p h n", p=P))):
                a.dma_start(dst, src).then_inc(S("tables").sem, 16)
            for t in range(nt):
                a.wait_ge(S("feat").sem, S("feat").at(t + 1))
                nc.scalar.activation(f_tok[:, t, :], PS[t % 2][:, 0:512], ACT.Copy).then_inc(S("f_tok").sem, 1)
                a.wait_ge(S("f_tok").sem, S("f_tok").up())
            for h in range(2):
                a.wait_ge(S("z").sem, S("z").at(h + 1))
                nc.scalar.activation(f_z[:, h, 0:n], PS[2 + h][:, 0:n], ACT.Copy).then_inc(S("f_z").sem, 1)
                a.wait_ge(S("f_z").sem, S("f_z").up())
            for m in range(2):
                a.wait_ge(S("mixed").sem, S("mixed").at(m + 1))
                nc.scalar.activation(a_hi[:, m, 0:n], PS[m][:, 0:n], ACT.Copy).then_inc(S("high").sem, 1)
                a.wait_ge(S("high").sem, S("high").up())

        def four_dve(v, st, l):
            S = lambda n: local(st, n)
            n = P * (NX if l == LAYERS - 1 else NT)
            for m in range(2):
                v.wait_ge(S("high").sem, S("high").at(m + 1))
                nc.vector.tensor_tensor(a_lo[:, m, 0:n], PS[m][:, 0:n], a_hi[:, m, 0:n].bitcast(F32), ALU.subtract).then_inc(v_step.sem, 1)
                v.wait_ge(v_step.sem, v_step.up())

        def rope_tiles(l):
            own = SEQ if l == LAYERS - 1 else TOK
            return [(2 + i, own) for i in range(4)] + [(6, TOK)]

        def rope_pe(p, st, l):
            S = lambda n: local(st, n)
            tiles = rope_tiles(l)
            p.wait_ge(S("tables").sem, S("tables").at(64))
            for j, (tile, n) in enumerate(tiles):
                p.wait_ge(S("squared").sem, S("squared").at(j + 1))
                if j >= 1:
                    if j > 0:
                        p.wait_ge(S("root").sem, S("root").at(j))
                for lo in range(0, n, 512):
                    hi = min(n, lo + 512)
                    mm = p.matmul(PS[0][:, lo:hi], head_mean[:], r_sq[:, j % 2, lo:hi], start=True, stop=True)
                mm.then_inc(S("means").sem, 1)
                p.wait_ge(S("normed").sem, S("normed").at(j + 1))
                if j >= 1:
                    if j > 0:
                        p.wait_ge(S("sines").sem, S("sines").at(j))
                p.matmul(PS[1][:, 0:SEQ], turn[:], proj[:, tile, 0:SEQ], start=True, stop=True).then_inc(S("quarter").sem, 1)
            if len(tiles) > 0:
                p.wait_ge(S("rotated").sem, S("rotated").at(len(tiles)))
            for lo, hi in ((0, 512), (512, TOK)):
                mm = p.matmul(PS[2][:, lo:hi], swap[:], proj[:, 6, lo:hi], start=True, stop=True)
            mm.then_inc(S("swapped").sem, 1)

        def rope_act(a, st, l):
            S = lambda n: local(st, n)
            a.dma_start(r_cos[:], dram["cos"]).then_inc(S("tables").sem, 16)
            a.dma_start(r_sin[:], dram["sin"]).then_inc(S("tables").sem, 16)
            a.dma_start(turn[:], dram["turn"]).then_inc(S("tables").sem, 16)
            a.dma_start(swap[:], dram["swap"]).then_inc(S("tables").sem, 16)
            for j, (tile, n) in enumerate(rope_tiles(l)):
                if j - 1 > 0:
                    a.wait_ge(S("means").sem, S("means").at(j - 1))
                nc.scalar.activation(r_sq[:, j % 2, 0:n], proj[:, tile, 0:n], ACT.Square).then_inc(S("squared").sem, 1)
                a.wait_ge(S("squared").sem, S("squared").up())
                a.wait_ge(S("means").sem, S("means").at(j + 1))
                if j > 0:
                    a.wait_ge(S("normed").sem, S("normed").at(j))
                nc.scalar.activation(r_std[:, 0:n], PS[0][:, 0:n], ACT.Sqrt, bias=eps).then_inc(S("root").sem, 1)
                a.wait_ge(S("root").sem, S("root").up())
            a.wait_ge(S("swapped").sem, S("swapped").at(1))
            nc.scalar.activation(k_swap[:], PS[2][:, 0:TOK], ACT.Copy).then_inc(a_step.sem, 1)
            a.wait_ge(a_step.sem, a_step.up())

        def rope_dve(v, st, l):
            S = lambda n: local(st, n)
            v.wait_ge(S("tables").sem, S("tables").at(64))
            for j, (tile, n) in enumerate(rope_tiles(l)):
                v.wait_ge(S("root").sem, S("root").at(j + 1))
                nc.vector.reciprocal(r_std[:, 0:n], r_std[:, 0:n]).then_inc(v_step.sem, 1)
                v.wait_ge(v_step.sem, v_step.up())
                gain = col("kn", l) if tile == 6 else qn_scaled[:, l:l + 1]
                nc.vector.scalar_tensor_tensor(proj[:, tile, 0:n], proj[:, tile, 0:n], gain, r_std[:, 0:n],
                                                    ALU.mult, ALU.mult).then_inc(S("normed").sem, 1)
                v.wait_ge(S("normed").sem, S("normed").up())
                v.wait_ge(S("quarter").sem, S("quarter").at(j + 1))
                nc.vector.tensor_tensor(r_tmp[:], PS[1][:, 0:SEQ], r_sin[:], ALU.mult).then_inc(S("sines").sem, 1)
                v.wait_ge(S("sines").sem, S("sines").up())
                nc.vector.tensor_tensor(proj[:, tile, 0:SEQ], proj[:, tile, 0:SEQ], r_cos[:], ALU.mult).then_inc(v_step.sem, 1)
                v.wait_ge(v_step.sem, v_step.up())
                nc.vector.tensor_tensor(proj[:, tile, 0:SEQ], proj[:, tile, 0:SEQ], r_tmp[:], ALU.add).then_inc(S("rotated").sem, 1)
                v.wait_ge(S("rotated").sem, S("rotated").up())

        qn_scaled = small[:, 44:46]

        gla = Scan("gla")
        scans = {(l, b): Scan("hg", back=b, l=l) for l in range(LAYERS) for b in (False, True)}
        att1 = attention_plan("first")
        att2 = [attention_plan("second", l) for l in range(LAYERS)]

        @block.tensor
        def _(p):
            p.wait_ge(s_load.sem, 16 * N_CONST)
            p.wait_ge(s_setup.sem, 1)
            for lo, hi in ((0, 512), (512, STRIP)):
                mm = p.matmul(PS[0][0:12, lo:hi], rel[:], onehot[:, lo:hi], start=True, stop=True)
            mm.then_inc(local(("setup", 0), "bias").sem, 1)
            stage_end(p, "pe")
            norm_pe(p, ("norm", 0), "x")
            stage_end(p, "pe")
            gemm_pe(p, "in1")
            stage_end(p, "pe")
            gates_pe(p, ("scan", 0), gla)
            levels_pe(p, ("scan", 0), gla)
            state_pe(p, ("scan", 0), gla)
            stage_end(p, "pe")
            read_pe(p, ("read", 0), SEQ)
            stage_end(p, "pe")
            att_pe(p, ("att", 0), *att1)
            stage_end(p, "pe")
            gemm_pe(p, "out1")
            stage_end(p, "pe")
            norm_pe(p, ("norm", 1), "x")
            stage_end(p, "pe")
            for g in range(4):
                gemm_pe(p, f"ff1_{g}")
            stage_end(p, "pe")
            norm_pe(p, ("norm", 2), "x")
            stage_end(p, "pe")
            for l in range(LAYERS):
                norm_pe(p, ("norm", 3 + 2 * l), norm_plan("mod_a", l)[0])
                stage_end(p, "pe")
                gemm_pe(p, f"in2_{l}")
                stage_end(p, "pe")
                for b in (False, True):
                    s = scans[l, b]
                    st = ("scan", 1 + 2 * l + int(b))
                    levels_pe(p, st, s)
                    state_pe(p, st, s)
                    stage_end(p, "pe")
                read_pe(p, ("read", 1 + l), s.own)
                stage_end(p, "pe")
                four_pe(p, ("four", l), l)
                stage_end(p, "pe")
                rope_pe(p, ("rope", l), l)
                stage_end(p, "pe")
                att_pe(p, ("att", 1 + l), *att2[l])
                stage_end(p, "pe")
                gemm_pe(p, f"out2_{l}")
                stage_end(p, "pe")
                norm_pe(p, ("norm", 4 + 2 * l), norm_plan("mod_f", l)[0])
                stage_end(p, "pe")
                for g in range(3):
                    gemm_pe(p, f"ff2_{l}_{g}")
                stage_end(p, "pe")
            norm_pe(p, ("norm", 7), "x")
            stage_end(p, "pe")

        @block.scalar
        def _(act):
            a = act
            act.wait_ge(s_load.sem, 16 * N_CONST)
            act.dma_start(w_a2[:], dram["w_a2"]).then_inc(s_wa2.sem, 16)
            o = COLS["c"][0]
            nc.scalar.activation(silu_c[:].rearrange("p k c -> p (k c)"), cols[:, o:o + 16], ACT.Silu).then_inc(s_setup_a.sem, 1)
            a.wait_ge(s_setup_a.sem, s_setup_a.up())
            a.wait_ge(s_setup.sem, s_setup.at(2))
            nc.scalar.activation(small[:, 48:52], small[:, 48:52], ACT.Sigmoid).then_inc(s_setup_a.sem, 1)
            a.wait_ge(s_setup_a.sem, s_setup_a.up())
            act_split(a, 0)
            a.wait_ge(local(("setup", 0), "bias_out").sem, local(("setup", 0), "bias_out").at(1))
            act.dma_start(bias_dram[:, :, :], bias_row[:].unsqueeze(1).to_broadcast([12, P, STRIP])).then_inc(s_load_bias.sem, 16)
            a.wait_ge(s_load_bias.sem, s_load_bias.at(16))
            stage_end(a, "act")
            norm_act(a, ("norm", 0), "x", norm_plan("norm1")[1])
            stage_end(a, "act")
            gemm_act(a, "in1")
            stage_end(a, "act")
            gates_act(a, ("scan", 0), gla)
            levels_act(a, ("scan", 0), gla)
            state_act(a, ("scan", 0), gla)
            stage_end(a, "act")
            read_act(a, ("read", 0), proj1[:, 6:8, :], proj1[:, 8:10, :], SEQ, 3)
            stage_end(a, "act")
            att_act(a, ("att", 0), *att1)
            stage_end(a, "act")
            gemm_act(a, "out1")
            stage_end(a, "act")
            norm_act(a, ("norm", 1), "x", norm_plan("norm2")[1])
            stage_end(a, "act")
            for g in range(4):
                gemm_act(a, f"ff1_{g}")
            stage_end(a, "act")
            act.dma_start(xc[:], dram["xc"]).then_inc(local(("load", 0), "ctx").sem, 16)
            norm_act(a, ("norm", 2), "x", None)
            a.wait_ge(local(("load", 0), "ctx").sem, local(("load", 0), "ctx").at(16))
            stage_end(a, "act")
            for l in range(LAYERS):
                norm_act(a, ("norm", 3 + 2 * l), *norm_plan("mod_a", l))
                stage_end(a, "act")
                gemm_act(a, f"in2_{l}")
                stage_end(a, "act")
                for b in (False, True):
                    s = scans[l, b]
                    st = ("scan", 1 + 2 * l + int(b))
                    gates_act(a, st, s)
                    levels_act(a, st, s)
                    state_act(a, st, s)
                    stage_end(a, "act")
                read_act(a, ("read", 1 + l), proj[:, 7:9, 0:s.own], proj[:, 13:15, 0:s.own], s.own, 6)
                stage_end(a, "act")
                four_act(a, ("four", l), l)
                stage_end(a, "act")
                rope_act(a, ("rope", l), l)
                stage_end(a, "act")
                att_act(a, ("att", 1 + l), *att2[l])
                stage_end(a, "act")
                gemm_act(a, f"out2_{l}")
                stage_end(a, "act")
                norm_act(a, ("norm", 4 + 2 * l), *norm_plan("mod_f", l))
                stage_end(a, "act")
                for g in range(3):
                    gemm_act(a, f"ff2_{l}_{g}")
                stage_end(a, "act")
            norm_act(a, ("norm", 7), "x", None)
            for k in range(KT):
                a.wait_ge(local(("norm", 7), "done").sem, local(("norm", 7), "done").at(k + 1))
                act.dma_start(out_t[k * P:(k + 1) * P, :], x[:, k, :]).then_inc(s_out.sem, 16)
            a.wait_ge(s_out.sem, s_out.at(16 * KT))
            stage_end(a, "act")

        @block.vector
        def _(dve):
            v = dve
            nc.vector.memset(small[:], 0.0).then_inc(v_step.sem, 1)
            v.wait_ge(v_step.sem, v_step.up())
            nc.vector.memset(eps, EPS).then_inc(v_step.sem, 1)
            v.wait_ge(v_step.sem, v_step.up())
            nc.vector.memset(one, 1.0).then_inc(v_step.sem, 1)
            v.wait_ge(v_step.sem, v_step.up())
            nc.vector.memset(lbs[:], 0.0).then_inc(v_step.sem, 1)
            v.wait_ge(v_step.sem, v_step.up())
            nc.vector.memset(lbs[:, :, :, :, 1:2], 1.0).then_inc(v_step.sem, 1)
            v.wait_ge(v_step.sem, v_step.up())
            nc.vector.memset(ones[:], 1.0).then_inc(s_setup.sem, 1)
            v.wait_ge(s_setup.sem, s_setup.up())
            v.wait_ge(s_load.sem, s_load.at(16 * N_CONST))
            o = COLS["lb"][0]
            lbv = cols[:, o:o + 8].rearrange("p (d l h) -> p d l h", d=2, l=2)
            sg = small[:, 48:52].rearrange("p (d h) -> p d h", d=2)
            nc.vector.tensor_tensor(sg, lbv[:, :, 1, :], lbv[:, :, 0, :], ALU.subtract).then_inc(s_setup.sem, 1)
            v.wait_ge(s_setup.sem, s_setup.up())
            nc.vector.tensor_scalar(qn_scaled, cols[:, COLS["qn"][0]:COLS["qn"][0] + 2], HD ** -0.5, None, ALU.mult).then_inc(v_step.sem, 1)
            v.wait_ge(v_step.sem, v_step.up())
            v.wait_ge(s_setup_a.sem, s_setup_a.at(2))
            nc.vector.tensor_copy(lbs[:, 1, :, :, 0], sg).then_inc(v_step.sem, 1)
            v.wait_ge(v_step.sem, v_step.up())
            nc.vector.tensor_scalar(lbs[:, 1, :, :, 1], sg, -1.0, 1.0, ALU.mult, ALU.add).then_inc(v_step.sem, 1)
            v.wait_ge(v_step.sem, v_step.up())
            v.wait_ge(local(("setup", 0), "bias").sem, local(("setup", 0), "bias").at(1))
            nc.vector.tensor_tensor(bias_row[:], PS[0][0:12, 0:STRIP], bias_add[:], ALU.add).then_inc(local(("setup", 0), "bias_out").sem, 1)
            v.wait_ge(local(("setup", 0), "bias_out").sem, local(("setup", 0), "bias_out").up())
            stage_end(v, "dve")
            norm_dve(v, ("norm", 0), "x", norm_plan("norm1")[1])
            stage_end(v, "dve")
            gemm_dve(v, "in1")
            stage_end(v, "dve")
            gates_dve(v, ("scan", 0), gla)
            levels_dve(v, ("scan", 0), gla)
            state_dve(v, ("scan", 0), gla)
            scan_out_dve(v, ("scan", 0), gla, proj1[:, 6:8, :], False)
            stage_end(v, "dve")
            read_dve(v, ("read", 0), proj1[:, 6:8, :], lambda h: col("gla_norm", h), SEQ, 3)
            stage_end(v, "dve")
            att_dve(v, ("att", 0), *att1)
            stage_end(v, "dve")
            gemm_dve(v, "out1")
            stage_end(v, "dve")
            norm_dve(v, ("norm", 1), "x", norm_plan("norm2")[1])
            stage_end(v, "dve")
            for g in range(4):
                gemm_dve(v, f"ff1_{g}")
            stage_end(v, "dve")
            final_dve(v, ("norm", 2), "final1")
            if len(ada) > 0:
                v.wait_ge(s_adao.sem, s_adao.at(len(ada)))
            for l in range(LAYERS):
                for c0 in (8, 32):
                    w = mods[:, l, c0:c0 + 8, :]
                    nc.vector.tensor_scalar(w, w, 1.0, None, ALU.add).then_inc(v_step.sem, 1)
                    v.wait_ge(v_step.sem, v_step.up())
            stage_end(v, "dve")
            for l in range(LAYERS):
                norm_dve(v, ("norm", 3 + 2 * l), *norm_plan("mod_a", l))
                stage_end(v, "dve")
                gemm_dve(v, f"in2_{l}", l)
                stage_end(v, "dve")
                for b in (False, True):
                    s = scans[l, b]
                    st = ("scan", 1 + 2 * l + int(b))
                    gates_dve(v, st, s)
                    levels_dve(v, st, s)
                    state_dve(v, st, s)
                    scan_out_dve(v, st, s, proj[:, 7:9, :], b)
                    stage_end(v, "dve")
                read_dve(v, ("read", 1 + l), proj[:, 7:9, 0:s.own], lambda h: col("hgn", l), s.own, 6)
                stage_end(v, "dve")
                four_dve(v, ("four", l), l)
                stage_end(v, "dve")
                rope_dve(v, ("rope", l), l)
                stage_end(v, "dve")
                att_dve(v, ("att", 1 + l), *att2[l])
                stage_end(v, "dve")
                gemm_dve(v, f"out2_{l}", l)
                stage_end(v, "dve")
                norm_dve(v, ("norm", 4 + 2 * l), *norm_plan("mod_f", l))
                stage_end(v, "dve")
                for g in range(3):
                    gemm_dve(v, f"ff2_{l}_{g}", l)
                stage_end(v, "dve")
            final_dve(v, ("norm", 7), "final2")
            stage_end(v, "dve")


def constants():
    f = np.float32
    c = {"ident": np.eye(P, dtype=f)}
    blk = np.kron(np.eye(2), np.ones((HD, HD)))
    c["head_mean"] = (blk / HD).astype(f)
    half = HD // 2
    q = half // 2
    r = np.zeros((HD, HD))
    for a in range(2):
        for i in range(q):
            r[a * half + i, a * half + q + i] = -1.0
            r[a * half + q + i, a * half + i] = 1.0
    c["turn"] = np.kron(np.eye(2), r).T.astype(f)
    c["swap"] = np.kron(np.array([[0, 1], [1, 0]]), np.eye(HD)).astype(f)
    s, t = np.arange(P)[:, None], np.arange(P)[None, :]
    m = np.zeros((P, 2, 4, P), np.int32)
    for i, b in enumerate((64, 32, 16)):
        same = s // (2 * b) == t // (2 * b)
        left, right = (s // b) % 2 == 0, (t // b) % 2 == 1
        m[:, 0, i] = same & left & right
        m[:, 1, i] = (same & left & right).T
    m[:, 0, 3] = (s // SUB == t // SUB) & (s <= t)
    m[:, 1, 3] = m[:, 0, 3].T
    c["masks"] = m
    rs = np.ones((P, TOK), f)
    rs[:, ::P] = 0.0
    c["reset"] = rs
    dist = SEQ - 1 - np.arange(STRIP)
    n = np.maximum(dist, 0)
    exact = BUCKETS // 2
    logv = np.log(np.maximum(n, 1).astype(f) / f(exact)) / f(math.log(MAX_DIST / exact))
    large = np.minimum(exact + (logv * f(BUCKETS - exact)).astype(np.int32), BUCKETS - 1)
    bucket = np.where(n < exact, n, large)
    c["onehot"] = (np.arange(BUCKETS)[:, None] == bucket[None, :]).astype(f)
    seen = (dist <= 128).astype(int) + (dist % 4 == 0) + (dist % 16 == 0)
    add_a = np.where((dist >= 0) & (seen > 0), np.log(np.maximum(seen, 1)), NEG)
    add_c = np.where(dist >= 0, 0.0, NEG)
    c["bias_add"] = np.stack([add_a] * 6 + [add_c] * 6).astype(f)
    pos = np.arange(SEQ)
    freqs = (10000.0 ** (-np.arange(0, half, 2, dtype=f) / f(half))).astype(f)
    ang = np.stack([(pos // 64).astype(f)[None, :] * freqs[:, None], (pos % 64).astype(f)[None, :] * freqs[:, None]])
    ang = np.concatenate([ang[0], ang[0], ang[1], ang[1]])
    c["cos"] = np.tile(np.cos(ang), (2, 1)).astype(f)
    c["sin"] = np.tile(np.sin(ang), (2, 1)).astype(f)

    def table(n):
        a = 2 * np.pi * np.outer(np.arange(n), np.arange(n)) / n
        return np.cos(a) / math.sqrt(n), np.sin(a) / math.sqrt(n)

    cs, sn = table(HD)
    c["f_feat"] = np.concatenate([np.kron(np.eye(2), cs), np.kron(np.eye(2), sn)], 1).astype(f)
    for n, name in ((SEQ, "f_tab"), (CTX, "f_tab_c")):
        cs, sn = table(n)
        c[name] = np.concatenate([cs.reshape(n // P, P, n), -sn.reshape(n // P, P, n)]).transpose(1, 0, 2).astype(f)
    return c


def kernel(**inputs):
    import numpy as _np
    import concourse.bacc as _bacc
    from concourse import mybir as _mybir
    from concourse.bass_utils import run_bass_kernel_spmd as _run

    g = {k: _np.asarray(v) for k, v in inputs.items()}
    feat = lambda a: _np.asarray(a).reshape(-1, P).T
    per_head = lambda a: _np.tile(a.T, (2, 1))
    packed = {
        "norm1": feat(g["norm1_w"][0]), "norm2": feat(g["norm2_w"][0]), "final1": feat(g["final_norm_w"]),
        "final2": feat(g["final_norm_2"]), "gla_b": feat(g["gla_b_a"][0]), "gla_norm": feat(g["gla_norm_w"][0]),
        "qn": per_head(g["q_norm_2"]), "kn": per_head(g["k_norm_2"]), "hgn": per_head(g["hg_norm_2"]),
        "lb": feat(g["hg_lb_logits_2"]), "b_ada": feat(g["b_ada_2"]),
        "c": _np.stack([feat(g["c_2"][0]), feat(g["c_ctx_2"])], 2).reshape(P, 16),
    }
    arrays = {
        "x": g["x"][0].T.reshape(KT, P, SEQ).transpose(1, 0, 2),
        "xc": g["ctx_2"][0].T.reshape(KT, P, CTX).transpose(1, 0, 2),
        "cols": _np.concatenate([packed[n] for n in COLS], 1),
        "rel": g["rel_bias"], "w_a2": g["gla_w_a2"][0], "w_in": g["w_in"][0], "w_out": g["w_out"][0],
        "w_ff1": g["w_ff1"][0], "w_ff2": g["w_ff2"][0],
    }
    for l in range(LAYERS):
        arrays |= {f"w_in2_{l}": g["w_in_2"][l], f"w_out2_{l}": g["w_out_2"][l], f"w_gate_{l}": g["w_gate_2"][l],
                   f"w_up_{l}": g["w_up_2"][l], f"w_down_{l}": g["w_down_2"][l], f"w_ada_{l}": g["w_ada_2"][l],
                   f"w_four_{l}": g["w_four_2"][l]}
    arrays |= constants()
    nc = _bacc.Bacc("TRN2", target_bir_lowering=False, num_devices=1)
    arrays = {f"in_{n}": _np.ascontiguousarray(a) for n, a in arrays.items()}
    dram = {n[3:]: nc.dram_tensor(n, a.shape, _mybir.dt.from_np(a.dtype), kind="ExternalInput").ap()
            for n, a in arrays.items()}
    out = nc.dram_tensor("out_t", (D, SEQ), _mybir.dt.float32, kind="ExternalOutput").ap()
    blocks_kernel(nc, dram, out)
    r = _run(nc, [arrays], core_ids=[0])
    return _np.ascontiguousarray(_np.asarray(r.results[0]["out_t"]).T)[None]
```
